# Optimizing a Trainium2 kernel written in Bass

```python
import jax
import jax.numpy as jnp
from jax import lax
import numpy as np

D_MODEL = 2048
BATCH = 1
SEQ = 256
DEPTH = 2

N_MIXERS = 4
DEEPNORM_ALPHA = (2.0 * DEPTH) ** 0.25
DEEPNORM_BETA = (8.0 * DEPTH) ** -0.25
LN_EPS = 1e-5
D_FF = 4 * D_MODEL
NEG_INF = -1e30

LRU_WIDTH = D_MODEL
LRU_BLOCKS = 8
LRU_BLOCK_W = LRU_WIDTH // LRU_BLOCKS
CONV_WIDTH = 4
LRU_C = 8.0

ATTN_HEAD_DIM = 128
ATTN_HEADS = D_MODEL // ATTN_HEAD_DIM
MOBA_BLOCK = 256
MOBA_TOPK = 3
MOBA_Q_CHUNK = 16
ROPE_THETA = 500000.0
ROPE_DIM = ATTN_HEAD_DIM // 4

RWKV_HEAD_DIM = 64
RWKV_HEADS = D_MODEL // RWKV_HEAD_DIM
RWKV_DECAY_LORA = 96
RWKV_AAA_LORA = 96
RWKV_GATE_LORA = 256
RWKV_LNX_EPS = 64e-5

POOL_WINDOWS = (2, 4, 8, 16)
POOL_GROUPS = len(POOL_WINDOWS)
POOL_GROUP_W = D_MODEL // POOL_GROUPS

kernel_name = "hybrid_rglru_moba_rwkv7_pool_deepnorm"

def _layers_of(mixer):
    return len(range(mixer, DEPTH, N_MIXERS))

def _layer_norm(x, g, b):
    x32 = x.astype(jnp.float32)
    mean = jnp.mean(x32, axis=-1, keepdims=True)
    var = jnp.mean(jnp.square(x32 - mean), axis=-1, keepdims=True)
    return ((x32 - mean) * lax.rsqrt(var + LN_EPS) * g + b).astype(x.dtype)

def _sqrelu_mlp(x, w1, w2):
    h = jax.nn.relu(x @ w1)
    return (h * h) @ w2

def _linear_recurrence_combine(left, right):
    a_l, b_l = left
    a_r, b_r = right
    return a_l * a_r, a_r * b_l + b_r

def _rglru_mixer(x, w_in, conv_w, conv_b, gate_a_w, gate_a_b, gate_x_w, gate_x_b, lam, w_out):
    bsz, seqlen, _ = x.shape
    gate, u = jnp.split(x @ w_in, 2, axis=-1)
    u = lax.conv_general_dilated(
        u, conv_w[:, None, :], window_strides=(1,), padding=[(CONV_WIDTH - 1, 0)],
        dimension_numbers=("NWC", "WIO", "NWC"), feature_group_count=LRU_WIDTH) + conv_b
    ub = u.reshape(bsz, seqlen, LRU_BLOCKS, LRU_BLOCK_W)
    r = jax.nn.sigmoid((jnp.einsum("bsnw,nwv->bsnv", ub, gate_a_w) + gate_a_b).astype(jnp.float32))
    i = jax.nn.sigmoid((jnp.einsum("bsnw,nwv->bsnv", ub, gate_x_w) + gate_x_b).astype(jnp.float32))
    log_a = -LRU_C * r * jax.nn.softplus(-lam.astype(jnp.float32)).reshape(LRU_BLOCKS, LRU_BLOCK_W)
    a = jnp.exp(log_a)
    b = ub.astype(jnp.float32) * i * jnp.sqrt(-jnp.expm1(2.0 * log_a))
    _, h = lax.associative_scan(_linear_recurrence_combine, (a, b), axis=1)
    h = h.reshape(bsz, seqlen, LRU_WIDTH).astype(x.dtype)
    return (jax.nn.gelu(gate) * h) @ w_out

def _partial_rope(t, cos, sin):
    half = ROPE_DIM // 2
    t32 = t.astype(jnp.float32)
    t1, t2 = t32[..., :half], t32[..., half:ROPE_DIM]
    c, s = cos[None, :, None, :], sin[None, :, None, :]
    return jnp.concatenate([t1 * c - t2 * s, t2 * c + t1 * s, t32[..., ROPE_DIM:]], axis=-1).astype(t.dtype)

def _moba_mixer(x, w_qkv, w_out):
    bsz, seqlen, _ = x.shape
    n_blk = -(-seqlen // MOBA_BLOCK)
    pad = n_blk * MOBA_BLOCK - seqlen
    top_k = min(MOBA_TOPK, n_blk)
    qkv = (x @ w_qkv).reshape(bsz, seqlen, 3, ATTN_HEADS, ATTN_HEAD_DIM)
    q, k, v = qkv[:, :, 0], qkv[:, :, 1], qkv[:, :, 2]
    pos = jnp.arange(seqlen, dtype=jnp.float32)
    inv_freq = ROPE_THETA ** (-jnp.arange(0, ROPE_DIM, 2, dtype=jnp.float32) / ROPE_DIM)
    ang = pos[:, None] * inv_freq[None, :]
    cos, sin = jnp.cos(ang), jnp.sin(ang)
    q = (_partial_rope(q, cos, sin) * (ATTN_HEAD_DIM ** -0.5)).transpose(0, 2, 1, 3)
    k = _partial_rope(k, cos, sin).transpose(0, 2, 1, 3)
    v = v.transpose(0, 2, 1, 3)
    blk_shape = (bsz, ATTN_HEADS, n_blk, MOBA_BLOCK, ATTN_HEAD_DIM)
    k_blk = jnp.pad(k, ((0, 0), (0, 0), (0, pad), (0, 0))).reshape(blk_shape)
    v_blk = jnp.pad(v, ((0, 0), (0, 0), (0, pad), (0, 0))).reshape(blk_shape)
    k_mean = jnp.mean(k_blk.astype(jnp.float32), axis=3)
    gate = jnp.einsum("bhsd,bhnd->bhsn", q.astype(jnp.float32), k_mean)
    q_blk = jnp.arange(seqlen) // MOBA_BLOCK
    past = jnp.arange(n_blk)[None, :] < q_blk[:, None]
    gate = jnp.where(past, gate, NEG_INF)
    _, sel = lax.top_k(gate, top_k)
    sel_valid = sel < q_blk[:, None]
    b_idx = jnp.arange(bsz)[:, None, None, None]
    h_idx = jnp.arange(ATTN_HEADS)[None, :, None, None]
    key_off = jnp.arange(MOBA_BLOCK)
    n_sel = top_k * MOBA_BLOCK

    def chunk(c):
        start = c * MOBA_Q_CHUNK
        q_c = lax.dynamic_slice_in_dim(q, start, MOBA_Q_CHUNK, axis=2)
        sel_c = lax.dynamic_slice_in_dim(sel, start, MOBA_Q_CHUNK, axis=2)
        valid_c = lax.dynamic_slice_in_dim(sel_valid, start, MOBA_Q_CHUNK, axis=2)
        own = start // MOBA_BLOCK
        k_own = lax.dynamic_index_in_dim(k_blk, own, axis=2, keepdims=False)
        v_own = lax.dynamic_index_in_dim(v_blk, own, axis=2, keepdims=False)
        k_sel = k_blk[b_idx, h_idx, sel_c]
        v_sel = v_blk[b_idx, h_idx, sel_c]
        s_sel = jnp.einsum("bhcd,bhcjpd->bhcjp", q_c, k_sel, preferred_element_type=jnp.float32)
        s_sel = jnp.where(valid_c[..., None], s_sel, NEG_INF)
        s_own = jnp.einsum("bhcd,bhpd->bhcp", q_c, k_own, preferred_element_type=jnp.float32)
        q_pos = start + jnp.arange(MOBA_Q_CHUNK)
        k_pos = own * MOBA_BLOCK + key_off
        s_own = jnp.where(k_pos[None, :] <= q_pos[:, None], s_own, NEG_INF)
        s = jnp.concatenate([s_sel.reshape(bsz, ATTN_HEADS, MOBA_Q_CHUNK, n_sel), s_own], axis=-1)
        p = jax.nn.softmax(s, axis=-1).astype(v.dtype)
        p_sel = p[..., :n_sel].reshape(bsz, ATTN_HEADS, MOBA_Q_CHUNK, top_k, MOBA_BLOCK)
        p_own = p[..., n_sel:]
        return (jnp.einsum("bhcjp,bhcjpd->bhcd", p_sel, v_sel)
                + jnp.einsum("bhcp,bhpd->bhcd", p_own, v_own))

    o = lax.map(chunk, jnp.arange(seqlen // MOBA_Q_CHUNK))
    o = o.transpose(1, 0, 3, 2, 4).reshape(bsz, seqlen, ATTN_HEADS * ATTN_HEAD_DIM)
    return o @ w_out

def _token_shift(x):
    return jnp.pad(x, ((0, 0), (1, 0), (0, 0)))[:, :-1]

def _rwkv7_step(state, inp):
    r_t, w_t, k_t, v_t, kk_t, b_t = inp
    sa = jnp.einsum("bhvk,bhk->bhv", state, -kk_t)
    state = (state * w_t[:, :, None, :]
             + jnp.einsum("bhv,bhk->bhvk", sa, b_t)
             + jnp.einsum("bhv,bhk->bhvk", v_t, k_t))
    return state, jnp.einsum("bhvk,bhk->bhv", state, r_t)

def _rwkv7_mixer(x, mu, w_rkv, w0, w_w1, w_w2, a0, a_w1, a_w2, g_w1, g_w2,
                 k_k, k_a, r_k, lnx_g, lnx_b, w_out):
    f32 = jnp.float32
    bsz, seqlen, _ = x.shape
    hs = (bsz, seqlen, RWKV_HEADS, RWKV_HEAD_DIM)
    xx = _token_shift(x) - x
    x_rkv = x[:, :, None, :] + xx[:, :, None, :] * mu[:3]
    rkv = jnp.einsum("bsgd,gde->bsge", x_rkv, w_rkv)
    r, k, v = rkv[:, :, 0], rkv[:, :, 1], rkv[:, :, 2]
    xw = x + xx * mu[3]
    xa = x + xx * mu[4]
    xg = x + xx * mu[5]
    w_log = -jax.nn.softplus(-(w0 + jnp.tanh(xw @ w_w1) @ w_w2).astype(f32)) - 0.5
    decay = jnp.exp(-jnp.exp(w_log)).reshape(hs)
    a = jax.nn.sigmoid((a0 + (xa @ a_w1) @ a_w2).astype(f32))
    g = jax.nn.sigmoid(xg @ g_w1) @ g_w2
    kk = (k * k_k).astype(f32).reshape(hs)
    kk = kk / jnp.maximum(jnp.sqrt(jnp.sum(kk * kk, axis=-1, keepdims=True)), 1e-12)
    k32 = (k.astype(f32) * (1.0 + (a - 1.0) * k_a)).reshape(hs)
    r32 = r.astype(f32).reshape(hs)
    v32 = v.astype(f32).reshape(hs)
    b = kk * a.reshape(hs)
    xs = tuple(jnp.moveaxis(t, 1, 0) for t in (r32, decay, k32, v32, kk, b))
    state0 = jnp.zeros((bsz, RWKV_HEADS, RWKV_HEAD_DIM, RWKV_HEAD_DIM), f32)
    _, y = lax.scan(_rwkv7_step, state0, xs)
    y = jnp.moveaxis(y, 0, 1)
    mean = jnp.mean(y, axis=-1, keepdims=True)
    var = jnp.mean(jnp.square(y - mean), axis=-1, keepdims=True)
    y = ((y - mean) * lax.rsqrt(var + RWKV_LNX_EPS)).reshape(bsz, seqlen, D_MODEL) * lnx_g + lnx_b
    bonus = jnp.sum(r32 * k32 * r_k, axis=-1, keepdims=True) * v32
    y = y + bonus.reshape(bsz, seqlen, D_MODEL)
    return (y.astype(x.dtype) * g) @ w_out

def _pool_mixer(x, w_pool, pool_scale):
    bsz, seqlen, _ = x.shape
    x32 = x.astype(jnp.float32)
    csum = jnp.pad(jnp.cumsum(x32, axis=1), ((0, 0), (1, 0), (0, 0)))
    t = jnp.arange(seqlen)
    groups = []
    for gi, w in enumerate(POOL_WINDOWS):
        sl = slice(gi * POOL_GROUP_W, (gi + 1) * POOL_GROUP_W)
        upper = csum[:, 1:, sl]
        lower = jnp.pad(csum[:, :seqlen - w + 1, sl], ((0, 0), (w - 1, 0), (0, 0)))
        count = jnp.minimum(t + 1, w).astype(jnp.float32)[None, :, None]
        groups.append((upper - lower) / count - x32[:, :, sl])
    pooled = jnp.stack(groups, axis=2).astype(x.dtype)
    y = jnp.einsum("bsgc,gce->bsge", pooled, w_pool).reshape(bsz, seqlen, D_MODEL)
    return y * pool_scale

def setup_inputs(seed: int = 0) -> dict:
    key = jax.random.key(seed)
    keys = list(jax.random.split(key, 48))
    f32 = jnp.float32

    def nrm(shape, scale):
        return jax.random.normal(keys.pop(), shape, f32) * scale

    def uni(shape, lo, hi):
        return jax.random.uniform(keys.pop(), shape, f32, lo, hi)

    n_a, n_b, n_c, n_d = (_layers_of(m) for m in range(N_MIXERS))
    D, R = D_MODEL, LRU_WIDTH
    beta = DEEPNORM_BETA
    u = uni((n_a, R), 0.9, 0.999)
    a_base = u ** (1.0 / LRU_C)
    return {
        "x": nrm((BATCH, SEQ, D), 1.0),
        "ln_g": 1.0 + nrm((DEPTH, 2, D), 0.05),
        "ln_b": nrm((DEPTH, 2, D), 0.01),
        "mlp_w1": nrm((DEPTH, D, D_FF), D ** -0.5),
        "mlp_w2": nrm((DEPTH, D_FF, D), D_FF ** -0.5 * beta),
        "rg_w_in": nrm((n_a, D, 2 * R), D ** -0.5),
        "rg_conv_w": nrm((n_a, CONV_WIDTH, R), CONV_WIDTH ** -0.5),
        "rg_conv_b": nrm((n_a, R), 0.01),
        "rg_gate_a_w": nrm((n_a, LRU_BLOCKS, LRU_BLOCK_W, LRU_BLOCK_W), LRU_BLOCK_W ** -0.5),
        "rg_gate_a_b": nrm((n_a, LRU_BLOCKS, LRU_BLOCK_W), 0.01),
        "rg_gate_x_w": nrm((n_a, LRU_BLOCKS, LRU_BLOCK_W, LRU_BLOCK_W), LRU_BLOCK_W ** -0.5),
        "rg_gate_x_b": nrm((n_a, LRU_BLOCKS, LRU_BLOCK_W), 0.01),
        "rg_lambda": jnp.log(a_base) - jnp.log1p(-a_base),
        "rg_w_out": nrm((n_a, R, D), R ** -0.5 * beta),
        "moba_w_qkv": nrm((n_b, D, 3 * D), D ** -0.5),
        "moba_w_out": nrm((n_b, D, D), D ** -0.5 * beta),
        "rwkv_mu": uni((n_c, 6, D), 0.0, 1.0),
        "rwkv_w_rkv": nrm((n_c, 3, D, D), D ** -0.5),
        "rwkv_w0": uni((n_c, D), -5.0, -1.0),
        "rwkv_w_w1": nrm((n_c, D, RWKV_DECAY_LORA), D ** -0.5),
        "rwkv_w_w2": nrm((n_c, RWKV_DECAY_LORA, D), 0.5 * RWKV_DECAY_LORA ** -0.5),
        "rwkv_a0": nrm((n_c, D), 0.3),
        "rwkv_a_w1": nrm((n_c, D, RWKV_AAA_LORA), D ** -0.5),
        "rwkv_a_w2": nrm((n_c, RWKV_AAA_LORA, D), 0.5 * RWKV_AAA_LORA ** -0.5),
        "rwkv_g_w1": nrm((n_c, D, RWKV_GATE_LORA), D ** -0.5),
        "rwkv_g_w2": nrm((n_c, RWKV_GATE_LORA, D), RWKV_GATE_LORA ** -0.5),
        "rwkv_k_k": 0.85 + nrm((n_c, D), 0.05),
        "rwkv_k_a": 1.0 + nrm((n_c, D), 0.05),
        "rwkv_r_k": nrm((n_c, RWKV_HEADS, RWKV_HEAD_DIM), 0.1),
        "rwkv_lnx_g": 1.0 + nrm((n_c, D), 0.05),
        "rwkv_lnx_b": nrm((n_c, D), 0.01),
        "rwkv_w_out": nrm((n_c, D, D), D ** -0.5 * beta),
        "pool_w": nrm((n_d, POOL_GROUPS, POOL_GROUP_W, POOL_GROUP_W), POOL_GROUP_W ** -0.5 * beta),
        "pool_scale": 1.0 + nrm((n_d, D), 0.05),
    }

def reference(x, ln_g, ln_b, mlp_w1, mlp_w2,
              rg_w_in, rg_conv_w, rg_conv_b, rg_gate_a_w, rg_gate_a_b, rg_gate_x_w, rg_gate_x_b,
              rg_lambda, rg_w_out,
              moba_w_qkv, moba_w_out,
              rwkv_mu, rwkv_w_rkv, rwkv_w0, rwkv_w_w1, rwkv_w_w2, rwkv_a0, rwkv_a_w1, rwkv_a_w2,
              rwkv_g_w1, rwkv_g_w2, rwkv_k_k, rwkv_k_a, rwkv_r_k, rwkv_lnx_g, rwkv_lnx_b, rwkv_w_out,
              pool_w, pool_scale):
    counts = [0] * N_MIXERS
    for layer in range(DEPTH):
        m = layer % N_MIXERS
        j = counts[m]
        counts[m] += 1
        if m == 0:
            y = _rglru_mixer(x, rg_w_in[j], rg_conv_w[j], rg_conv_b[j], rg_gate_a_w[j], rg_gate_a_b[j],
                             rg_gate_x_w[j], rg_gate_x_b[j], rg_lambda[j], rg_w_out[j])
        elif m == 1:
            y = _moba_mixer(x, moba_w_qkv[j], moba_w_out[j])
        elif m == 2:
            y = _rwkv7_mixer(x, rwkv_mu[j], rwkv_w_rkv[j], rwkv_w0[j], rwkv_w_w1[j], rwkv_w_w2[j],
                             rwkv_a0[j], rwkv_a_w1[j], rwkv_a_w2[j], rwkv_g_w1[j], rwkv_g_w2[j],
                             rwkv_k_k[j], rwkv_k_a[j], rwkv_r_k[j], rwkv_lnx_g[j], rwkv_lnx_b[j],
                             rwkv_w_out[j])
        else:
            y = _pool_mixer(x, pool_w[j], pool_scale[j])
        x = _layer_norm(DEEPNORM_ALPHA * x + y, ln_g[layer, 0], ln_b[layer, 0])
        x = _layer_norm(DEEPNORM_ALPHA * x + _sqrelu_mlp(x, mlp_w1[layer], mlp_w2[layer]),
                        ln_g[layer, 1], ln_b[layer, 1])
    return x


_drawn_inputs = setup_inputs


def setup_inputs(seed=0):
    import zlib

    import numpy as np

    out = dict(_drawn_inputs(seed))
    spreads = {}
    factors = {'ln_b': 2.737, 'rg_conv_b': 5.969, 'rg_gate_a_b': 200.0, 'rg_gate_x_b': 64.0}
    for name, (base, spread) in spreads.items():
        noise = np.random.default_rng([zlib.crc32(name.encode()), seed]).standard_normal(out[name].shape)
        drawn = base * np.exp(spread * noise) if base else spread * noise
        out[name] = jnp.asarray(drawn.astype(out[name].dtype))
    for name, factor in factors.items():
        out[name] = (out[name] * factor).astype(out[name].dtype)
    return out
```

```python
from contextlib import ExitStack

import numpy as np

import concourse.bass as bass
from concourse import mybir

F32 = mybir.dt.float32
F32R = mybir.dt.float32r
ALU = mybir.AluOpType
ACT = mybir.ActivationFunctionType
AX_X = mybir.AxisListType.X

P = 128
T = 256
D = 2048
NC = D // P
HALVES = T // P
GROUP = 4
NG = NC // GROUP
COLS = GROUP * P
KCH = 2
BLOCKS = NC // KCH
BLK = KCH * COLS
SPLITS = 4
AHEAD = 3
D_FF = 8192
SLABS = D_FF // D
LRU_BLOCKS = 8
LRU_W = D // LRU_BLOCKS
CONV = 4
LRU_C = 8.0
ROPE_HALF = 16
DEPTH = 2
ALPHA = (2.0 * DEPTH) ** 0.25
LN_EPS = 1e-5
QK_SCALE = 128 ** -0.5
NEG = -1e30

B_U = 0
B_GATES = B_U + NG * BLOCKS
B_G = B_GATES + BLOCKS
B_RO = B_G + NG * BLOCKS
B_MLP0 = B_RO + NG * BLOCKS
B_QKV = B_MLP0 + 2 * SLABS * NG * BLOCKS
B_MO = B_QKV + 3 * NG * BLOCKS
B_MLP1 = B_MO + NG * BLOCKS
B_END = B_MLP1 + 2 * SLABS * NG * BLOCKS
SLAB_BLOCKS = 2 * NG * BLOCKS

T_U, T_G, T_RO, T_MLP0, T_MO, T_MLP1 = 0, 4, 8, 12, 44, 48

R_X, R_CONV, R_RO, R_LN0, R_SQ0, R_LN1, R_ATT, R_LN2, R_SQ1 = 0, 4, 8, 12, 16, 32, 36, 40, 44

C_LNG, C_LNB, C_CONVW, C_CONVB, C_BA, C_BX, C_LAM = 0, 64, 128, 192, 208, 224, 240


def build_trunk(nc, x, ln_g, ln_b, mlp_w1, mlp_w2, rg_w_in, rg_conv_w, rg_conv_b, rg_gate_a_w,
                rg_gate_a_b, rg_gate_x_w, rg_gate_x_b, rg_lambda, rg_w_out, moba_w_qkv, moba_w_out,
                rope, out):
    with ExitStack() as ctx:
        def sb(name, shape, dt=F32):
            return ctx.enter_context(nc.sbuf_tensor(name, shape, dt))

        def sem(name):
            return ctx.enter_context(nc.semaphore(name))

        xin = sb("xin", [P, NC, 2, T], F32R)
        hid = sb("hid", [P, NC, 2, T], F32R)
        acc = sb("acc", [P, NC, T])
        f1 = sb("f1", [P, NC * T])
        f2 = sb("f2", [P, NC * T])
        f3 = sb("f3", [P, NC * T])
        e1 = sb("e1", [P, GROUP, T])
        e2 = sb("e2", [P, GROUP, T])
        wst = sb("wst", [P, BLOCKS, BLK])
        wh = sb("wh", [P, SPLITS, BLK], F32R)
        wl = sb("wl", [P, SPLITS, BLK], F32R)
        prm = sb("prm", [P, 256])
        ident = sb("ident", [P, P])
        ones = sb("ones", [P, P])
        eps = sb("eps", [P, 1])
        maskt = sb("maskt", [P, 3 * P])
        ropet = sb("ropet", [32, 2, T])
        small = sb("small", [P, 8, NC])
        stat = sb("stat", [P, 4, 8])
        ps = ctx.enter_context(nc.psum_tensor("ps", [P, 8, 512], F32))

        u3 = f1[:, :].rearrange("p (c t) -> p c t", t=T)
        r3 = f2[:, :].rearrange("p (c t) -> p c t", t=T)
        i3 = f3[:, :].rearrange("p (c t) -> p c t", t=T)
        qg = f1[:, 0:1024].rearrange("p (c t) -> p c t", t=T)
        kg = f1[:, 1024:2048].rearrange("p (c t) -> p c t", t=T)
        vg = f1[:, 2048:3072].rearrange("p (a n) -> p a n", a=HALVES)
        rot = f1[:, 3072:4096].rearrange("p (c t) -> p c t", t=T)
        cosd = f2[:, 3072:4096].rearrange("p (c t) -> p c t", t=T)
        prob = f2[:, 0:1536].rearrange("p (h n) -> p h n", n=3 * P)
        probt = f2[:, 1536:3072].rearrange("p (h n) -> p h n", n=3 * P)
        ln_sum, ln_mean, ln_std, ln_rstd = (f3[:, k * T:(k + 1) * T] for k in range(4))
        ln_sq = f3[:, 4 * T:8 * T].rearrange("p (g t) -> p g t", t=T)

        stage_full = [sem(f"stage_full{s}") for s in range(BLOCKS)]
        x_loaded = [sem(f"x_loaded{h}") for h in range(HALVES)]
        prm_loaded = sem("prm_loaded")
        wh_done = sem("wh_done")
        wl_done = sem("wl_done")
        mm_done = sem("mm_done")
        pair_ready = sem("pair_ready")
        psum_free = sem("psum_free")
        xt_done = sem("xt_done")
        xt_hi = sem("xt_hi")
        consts = sem("consts")
        prm_t = sem("prm_t")
        prm_ready = sem("prm_ready")
        sp_link = sem("sp_link")
        sp_abs = sem("sp_abs")
        sp_exp = sem("sp_exp")
        sp_ready = sem("sp_ready")
        hl_copied = sem("hl_copied")
        conv_link = sem("conv_link")
        conv_hi = sem("conv_hi")
        sig_done = sem("sig_done")
        at_done = sem("at_done")
        rec_link = sem("rec_link")
        rec_ratio = sem("rec_ratio")
        rec_root = sem("rec_root")
        h_ready = sem("h_ready")
        gelu_done = sem("gelu_done")
        prod_done = sem("prod_done")
        prod_hi = sem("prod_hi")
        acc_half = sem("acc_half")
        pool_sum = sem("pool_sum")
        acc_ready = sem("acc_ready")
        sq_hl = sem("sq_hl")
        sq_val = sem("sq_val")
        sq_hi = sem("sq_hi")
        ln_stepd = sem("ln_stepd")
        ln_mm = sem("ln_mm")
        ln_centred = sem("ln_centred")
        ln_squared = sem("ln_squared")
        ln_reduced = sem("ln_reduced")
        ln_root = sem("ln_root")
        ln_scaled = sem("ln_scaled")
        ln_value = sem("ln_value")
        ln_hi = sem("ln_hi")
        qk_link = sem("qk_link")
        qk_ready = sem("qk_ready")
        scores_done = sem("scores_done")
        att_link = sem("att_link")
        bias_ready = sem("bias_ready")
        exp_done = sem("exp_done")
        p_ready = sem("p_ready")
        v_stored = sem("v_stored")
        pt_done = sem("pt_done")
        pt_copied = sem("pt_copied")
        pv_done = sem("pv_done")
        pv_hi = sem("pv_hi")
        out_t = sem("out_t")
        out_copied = sem("out_copied")
        stored = sem("stored")

        def banks(half):
            return ps[:, 4 * half:4 * half + 4, :]

        def cols_of(w, first):
            return w.rearrange("(b k p) n -> b p k n", k=KCH, p=P)[:, :, :, bass.ds(first, COLS)]

        block = ctx.enter_context(nc.Block())

        @block.sync
        def _(sp):
            def load_block(src, kb, b):
                if b is not None:
                    sp.wait_ge(wl_done, b - (BLOCKS - 1))
                sp.dma_start(wst[:, kb, :].rearrange("p (k n) -> p k n", k=KCH), src)\
                  .then_inc(stage_full[kb], 16)

            def load_turn(w, col, b):
                col = sp.snap(col)
                src = cols_of(w, col)
                for kb in range(BLOCKS):
                    load_block(src[kb], kb, b + kb)

            for h in range(HALVES):
                sp.dma_start(f1[:, h * D:(h + 1) * D], x[0, h * P:(h + 1) * P, :])\
                  .then_inc(x_loaded[h], 16)
            w_in = rg_w_in[0]
            first = cols_of(w_in, D)
            for kb in range(BLOCKS):
                load_block(first[kb], kb, None)
            with sp.Fori(1, NG) as t:
                load_turn(w_in, D + t * COLS, B_U + t * BLOCKS)
            for gb in range(BLOCKS):
                w = (rg_gate_a_w, rg_gate_x_w)[(gb // 2) % 2]
                n0 = (gb // 4) * 4 + (gb % 2) * 2
                sp.wait_ge(wl_done, B_GATES + gb - (BLOCKS - 1))
                sp.dma_start(wst[:, gb, :].rearrange("p (k n) -> p k n", n=LRU_W),
                             w[0, n0:n0 + 2].rearrange("n (k p) v -> p (n k) v", p=P))\
                  .then_inc(stage_full[gb], 16)
            with sp.Fori(0, NG) as t:
                load_turn(w_in, t * COLS, B_G + t * BLOCKS)
            with sp.Fori(0, NG) as t:
                load_turn(rg_w_out[0], t * COLS, B_RO + t * BLOCKS)

            def load_mlp(layer, b0):
                with sp.Fori(0, SLABS) as s:
                    with sp.Fori(0, NG) as t:
                        load_turn(mlp_w1[layer], s * D + t * COLS,
                                  b0 + s * SLAB_BLOCKS + t * BLOCKS)
                    w2 = mlp_w2[layer].rearrange("(s r) n -> s r n", r=D)
                    with sp.Fori(0, NG) as t:
                        b = b0 + NG * BLOCKS + s * SLAB_BLOCKS + t * BLOCKS
                        slab = sp.snap(s + 0)
                        col = sp.snap(t * COLS)
                        for kb in range(BLOCKS):
                            src = w2[bass.ds(slab, 1), kb * KCH * P:(kb + 1) * KCH * P,
                                     bass.ds(col, COLS)]
                            load_block(src.rearrange("s (k p) n -> p (s k) n", p=P), kb, b + kb)

            load_mlp(0, B_MLP0)
            with sp.Fori(0, NG) as g:
                for part in range(3):
                    load_turn(moba_w_qkv[0], part * D + g * COLS,
                              B_QKV + (3 * g + part) * BLOCKS)
            with sp.Fori(0, NG) as t:
                load_turn(moba_w_out[0], t * COLS, B_MO + t * BLOCKS)
            load_mlp(1, B_MLP1)
            o3 = f2[:, :].rearrange("p (a n) -> p a n", a=HALVES)
            for g in range(NG):
                sp.wait_ge(out_copied, g + 1)
                sp.dma_start(out[0].rearrange("(a p) n -> p a n", p=P)[:, :, g * COLS:(g + 1) * COLS],
                             o3[:, :, g * COLS:(g + 1) * COLS]).then_inc(stored, 16)
            sp.wait_ge(stored, 16 * NG)

        @block.gpsimd
        def _(pool):
            pool.memset(ident[:, :], 0.0).then_inc(consts, 1)
            pool.memset(ones[:, :], 1.0 / D).then_inc(consts, 1)
            pool.memset(eps[:, :], LN_EPS).then_inc(consts, 1)
            pool.memset(maskt[:, :], 0.0).then_inc(consts, 1)
            pool.wait_ge(consts, 4)
            pool.affine_select(out=ident[:, :], in_=ident[:, :], compare_op=ALU.not_equal, fill=1.0,
                               base=0, pattern=[[-1, P]], channel_multiplier=1).then_inc(consts, 1)
            for lo, base, n in ((0, 0, P), (P, P, 2 * P)):
                pool.affine_select(out=maskt[:, lo:lo + n], in_=maskt[:, lo:lo + n],
                                   compare_op=ALU.is_ge, fill=NEG, base=base,
                                   pattern=[[-1, n]], channel_multiplier=1).then_inc(consts, 1)

            def residual(use, ready):
                for g in range(NG):
                    rows = slice(g * GROUP, (g + 1) * GROUP)
                    pool.wait_ge(pair_ready, ready + g + 1)
                    pool.tensor_tensor(acc[:, rows, :], xin[:, rows, 0, :], xin[:, rows, 1, :],
                                       ALU.add).then_inc(pool_sum, 1)
                    pool.wait_ge(pool_sum, use * NG + g + 1)
                    pool.tensor_scalar(acc[:, rows, :], acc[:, rows, :], ALPHA, None, ALU.mult)\
                        .then_inc(acc_ready, 1)

            residual(0, R_RO)
            residual(1, R_LN0)
            residual(2, R_LN1)
            residual(3, R_LN2)

        @block.tensor
        def _(pe):
            def turn(src, half, b, ready):
                dst = banks(half)
                for kb in range(BLOCKS):
                    if kb % 2 == 0:
                        pe.wait_ge(pair_ready, ready + kb // 2 + 1)
                    pe.wait_ge(wl_done, b + kb + 1)
                    s = kb % SPLITS
                    for kk in range(KCH):
                        c = kb * KCH + kk
                        for n in range(GROUP):
                            w = slice(kk * COLS + n * P, kk * COLS + (n + 1) * P)
                            pe.matmul(dst[:, n, :], wh[:, s, w], src[:, c, :, :],
                                      start=(c == 0), stop=False)
                            mm = pe.matmul(dst[:, n, 0:T], wl[:, s, w], src[:, c, 0, :],
                                           start=False, stop=(c == NC - 1))
                    mm.then_inc(mm_done, 1)

            def pair(src, b, ready, free):
                for j in range(2):
                    pe.wait_ge(psum_free, free + j + 1)
                    turn(src, j, b + j * BLOCKS, ready)

            def unit(src, b, ready, free):
                with pe.Fori(0, NG // 2) as h:
                    pair(src, b + h * (2 * BLOCKS), ready, free + h * 2)

            pe.wait_ge(consts, 5)
            for h in range(HALVES):
                pe.wait_ge(x_loaded[h], 16)
            for g in range(NG):
                for c in range(g * GROUP, (g + 1) * GROUP):
                    for h in range(HALVES):
                        mm = pe.transpose(ps[:, c // 2, (c % 2) * T + h * P:(c % 2) * T + (h + 1) * P],
                                          f1[:, h * D + c * P:h * D + (c + 1) * P], ident[:, :])
                mm.then_inc(xt_done, 1)
            pe.wait_ge(prm_loaded, 16 * 8)
            pe.wait_ge(psum_free, 1)
            for k in range(2):
                mm = pe.transpose(ps[:, 0, k * P:(k + 1) * P], f2[:, k * P:(k + 1) * P], ident[:, :])
            mm.then_inc(prm_t, 1)
            pe.wait_ge(prm_ready, 1)

            unit(xin, B_U, R_X, T_U)

            for gt in range(4):
                dst = banks(gt % 2)
                if gt < 2:
                    pe.wait_ge(psum_free, T_G + gt + 1)
                else:
                    pe.wait_ge(sig_done, gt - 1)
                pe.wait_ge(pair_ready, R_CONV + 2 * (gt // 2) + 2)
                for half in range(2):
                    gb = 2 * gt + half
                    pe.wait_ge(wl_done, B_GATES + gb + 1)
                    s = gb % SPLITS
                    for nl in range(2):
                        n = (gt // 2) * 4 + half * 2 + nl
                        for vc in range(2):
                            o = half * 4 + nl * 2 + vc
                            o_ap = dst[:, o // 2, (o % 2) * T:(o % 2 + 1) * T]
                            for kk in range(2):
                                w = slice((nl * 2 + kk) * LRU_W + vc * P, (nl * 2 + kk) * LRU_W + (vc + 1) * P)
                                c = 2 * n + kk
                                pe.matmul(o_ap, wh[:, s, w], hid[:, c, 0, :], start=(kk == 0), stop=False)
                                pe.matmul(o_ap, wh[:, s, w], hid[:, c, 1, :], start=False, stop=False)
                                mm = pe.matmul(o_ap, wl[:, s, w], hid[:, c, 0, :], start=False,
                                               stop=(kk == 1))
                    mm.then_inc(mm_done, 1)

            pe.wait_ge(sig_done, 3)
            with pe.Fori(0, NG // 2) as h:
                for j in range(2):
                    if j == 1:
                        pe.wait_ge(sig_done, 4)
                    pe.wait_ge(psum_free, T_G + h * 2 + j + 1)
                    turn(xin, j, B_G + h * (2 * BLOCKS) + j * BLOCKS, R_X)

            unit(hid, B_RO, R_RO, T_RO)

            n_mm = [0]

            def ln_sums():
                for sums in range(2):
                    if sums == 0:
                        pe.wait_ge(ln_stepd, 3 * (n_mm[0] // 2) + 1)
                        mm = pe.matmul(ps[:, 0, 0:T], ones[:, :], ln_sum, start=True, stop=True)
                    else:
                        for g in range(NG):
                            pe.wait_ge(ln_reduced, NG * (n_mm[0] // 2) + g + 1)
                            mm = pe.matmul(ps[:, 1, 0:T], ones[:, :], ln_sq[:, g, :],
                                           start=(g == 0), stop=(g == NG - 1))
                    mm.then_inc(ln_mm, 1)
                    n_mm[0] += 1

            def mlp(b0, ready_x, ready_h, free):
                with pe.Fori(0, SLABS) as s:
                    with pe.Fori(0, NG // 2) as h:
                        pair(xin, b0 + s * SLAB_BLOCKS + h * (2 * BLOCKS), ready_x, free + s * 8 + h * 2)
                    with pe.Fori(0, NG // 2) as h:
                        pair(hid, b0 + NG * BLOCKS + s * SLAB_BLOCKS + h * (2 * BLOCKS),
                             ready_h + s * NG, free + 4 + s * 8 + h * 2)

            ln_sums()
            mlp(B_MLP0, R_LN0, R_SQ0, T_MLP0)
            ln_sums()

            with pe.Fori(0, NG // 2) as it:
                for j in range(2):
                    g = it * 2 + j
                    X, Y = banks(j), banks(1 - j)
                    b = B_QKV + it * (6 * BLOCKS) + j * (3 * BLOCKS)
                    turn(xin, j, b, R_LN1)
                    pe.wait_ge(pair_ready, g + R_ATT)
                    turn(xin, 1 - j, b + BLOCKS, R_LN1)
                    pe.wait_ge(qk_ready, it * 4 + 2 * j + 1)
                    for kb in range(BLOCKS):
                        if kb == BLOCKS // 2:
                            pe.wait_ge(qk_ready, it * 4 + 2 * j + 2)
                            for h in range(GROUP):
                                pe.matmul(Y[:, h, 0:P], qg[:, h, 0:P], kg[:, h, 0:P], start=True, stop=True)
                                mm = pe.matmul(Y[:, h, P:3 * P], qg[:, h, P:T], kg[:, h, :],
                                               start=True, stop=True)
                            mm.then_inc(scores_done, 1)
                        pe.wait_ge(wl_done, b + 2 * BLOCKS + kb + 1)
                        s = kb % SPLITS
                        for kk in range(KCH):
                            c = kb * KCH + kk
                            w = slice(kk * COLS, (kk + 1) * COLS)
                            for a in range(HALVES):
                                tok = slice(a * P, (a + 1) * P)
                                pe.matmul(X[:, a, :], xin[:, c, 0, tok], wh[:, s, w], start=(c == 0), stop=False)
                                pe.matmul(X[:, a, :], xin[:, c, 1, tok], wh[:, s, w], start=False, stop=False)
                                mm = pe.matmul(X[:, a, :], xin[:, c, 0, tok], wl[:, s, w], start=False,
                                               stop=(c == NC - 1))
                        mm.then_inc(mm_done, 1)
                    pe.wait_ge(p_ready, g + 1)
                    for h in range(GROUP):
                        for k in range(3):
                            mm = pe.transpose(Y[:, h, k * P:(k + 1) * P], prob[:, h, k * P:(k + 1) * P],
                                              ident[:, :])
                        mm.then_inc(pt_done, 1)
                    pe.wait_ge(v_stored, g + 1)
                    for h in range(GROUP):
                        pe.wait_ge(pt_copied, it * (2 * GROUP) + j * GROUP + h + 1)
                        o_ap = X[:, 2 + h // 2, (h % 2) * T:(h % 2 + 1) * T]
                        pe.matmul(o_ap, vg[:, 0, h * P:(h + 1) * P], probt[:, h, 0:2 * P],
                                  start=True, stop=False)
                        mm = pe.matmul(o_ap[:, P:T], vg[:, 1, h * P:(h + 1) * P], probt[:, h, 2 * P:3 * P],
                                       start=False, stop=True)
                    mm.then_inc(pv_done, 1)

            unit(hid, B_MO, R_ATT, T_MO)
            ln_sums()
            mlp(B_MLP1, R_LN2, R_SQ1, T_MLP1)
            ln_sums()
            xo = f1[:, :].rearrange("p (c t) -> p c t", t=T)
            for g in range(NG):
                pe.wait_ge(ln_value, 3 * NG + g + 1)
                if g >= 2:
                    pe.wait_ge(out_copied, g - 1)
                for a in range(HALVES):
                    for k in range(GROUP):
                        mm = pe.transpose(banks(1)[:, 2 * (g % 2) + a, k * P:(k + 1) * P],
                                          xo[:, g * GROUP + k, a * P:(a + 1) * P], ident[:, :])
                mm.then_inc(out_t, 1)

        @block.scalar
        def _(act):
            act.dma_start(ropet[:, :, :], rope).then_inc(prm_loaded, 16)
            for dst, n, src in ((f2[0:64, 0:P], 64, ln_g), (f2[64:128, 0:P], 64, ln_b)):
                act.dma_start(dst, src.rearrange("a b (c p) -> (a b c) p", p=P)).then_inc(prm_loaded, 16)
            act.dma_start(f2[0:64, P:2 * P], rg_conv_w.rearrange("l k (c p) -> (l k c) p", p=P))\
               .then_inc(prm_loaded, 16)
            act.dma_start(f2[64:80, P:2 * P], rg_conv_b.rearrange("l (c p) -> (l c) p", p=P))\
               .then_inc(prm_loaded, 16)
            act.dma_start(f2[80:96, P:2 * P], rg_gate_a_b.rearrange("l n (c p) -> (l n c) p", p=P))\
               .then_inc(prm_loaded, 16)
            act.dma_start(f2[96:112, P:2 * P], rg_gate_x_b.rearrange("l n (c p) -> (l n c) p", p=P))\
               .then_inc(prm_loaded, 16)
            act.dma_start(f2[112:128, P:2 * P], rg_lambda.rearrange("l (c p) -> (l c) p", p=P))\
               .then_inc(prm_loaded, 16)

            def split_hi(b, turn_no, off):
                kb = off % BLOCKS
                act.wait_ge(stage_full[kb], turn_no * 16 + 16 * (off // BLOCKS + 1))
                if not (isinstance(b, int) and b + off < SPLITS):
                    act.wait_ge(mm_done, b + (off - (SPLITS - 1)))
                act.activation(wh[:, off % SPLITS, :], wst[:, kb, :], ACT.Copy).then_inc(wh_done, 1)

            def splits(b, turn_no, lo=AHEAD, hi=AHEAD + BLOCKS):
                for off in range(lo, hi):
                    split_hi(b, turn_no, off)

            def take_hl(half, b, dst, done):
                act.wait_ge(mm_done, b + BLOCKS)
                act.activation(dst, banks(half)[:, :, T:2 * T], ACT.Copy).then_inc(done, 1)

            for g in range(NG):
                act.wait_ge(xt_done, g + 1)
                act.activation(xin[:, g * GROUP:(g + 1) * GROUP, 0, :],
                               ps[:, 2 * g:2 * g + 2, :].rearrange("p b (c t) -> p (b c) t", t=T),
                               ACT.Copy).then_inc(xt_hi, 1)
            act.wait_ge(sp_abs, 1)
            act.activation(small[:, 1, :], small[:, 0, :], ACT.Exp, scale=-1.0).then_inc(sp_exp, 1)
            splits(0, 0, 0, AHEAD)
            for t in range(NG):
                b = B_U + t * BLOCKS
                rows = slice(t * GROUP, (t + 1) * GROUP)
                splits(b, t)
                take_hl(t % 2, b, u3[:, rows, :], hl_copied)
                act.wait_ge(conv_link, (t + 1) * CONV)
                act.activation(hid[:, rows, 0, :], e1[:, :, :], ACT.Copy).then_inc(conv_hi, 1)
            for gt in range(4):
                splits(B_GATES, B_GATES // BLOCKS, AHEAD + 2 * gt, AHEAD + 2 * gt + 2)
                act.wait_ge(mm_done, B_GATES + 2 * gt + 2)
                if gt == 0:
                    act.wait_ge(prm_ready, 1)
                dst, bias = ((r3, C_BA), (i3, C_BX))[gt % 2]
                for o in range(8):
                    c = (gt // 2) * 8 + o
                    sg = act.activation(dst[:, c, :], banks(gt % 2)[:, o // 2, (o % 2) * T:(o % 2 + 1) * T],
                                        ACT.Sigmoid, bias=prm[:, bias + c:bias + c + 1])
                sg.then_inc(sig_done, 1)
            act.wait_ge(sp_ready, 1)
            act.wait_ge(sig_done, 4)
            for t in range(NG):
                b = B_G + t * BLOCKS
                for c in range(t * GROUP, (t + 1) * GROUP):
                    act.activation(u3[:, c, :], r3[:, c, :], ACT.Exp, scale=small[:, 6, c:c + 1])
                for c in range(t * GROUP, (t + 1) * GROUP):
                    th = act.activation(r3[:, c, :], r3[:, c, :], ACT.Tanh, scale=small[:, 7, c:c + 1])
                th.then_inc(at_done, 1)
                splits(b, B_G // BLOCKS + t, AHEAD, AHEAD + 4)
                act.wait_ge(rec_ratio, t + 1)
                act.activation(e1[:, :, :], e1[:, :, :], ACT.Sqrt, scale=2.0).then_inc(rec_root, 1)
                splits(b, B_G // BLOCKS + t, AHEAD + 4)
                take_hl(t % 2, b, acc[:, t * GROUP:(t + 1) * GROUP, :], hl_copied)
            for g in range(NG):
                rows = slice(g * GROUP, (g + 1) * GROUP)
                act.wait_ge(psum_free, 2 + T_G + g + 1)
                act.activation(acc[:, rows, :], acc[:, rows, :], ACT.Gelu_apprx_tanh).then_inc(gelu_done, 1)
                act.wait_ge(prod_done, g + 1)
                act.activation(hid[:, rows, 0, :], (e1, e2)[g % 2][:, :, :], ACT.Copy).then_inc(prod_hi, 1)

            def plain_unit(b0):
                with act.Fori(0, NG // 2) as h:
                    for j in range(2):
                        splits(b0 + h * (2 * BLOCKS) + j * BLOCKS, b0 // BLOCKS + h * 2 + j)

            n_ln = [0]

            def layer_norm(last=False):
                n = n_ln[0]
                n_ln[0] += 1
                for g in range(NG):
                    act.wait_ge(ln_centred, n * NG + g + 1)
                    if g >= 2:
                        act.wait_ge(ln_reduced, n * NG + g - 1)
                    act.activation((e1, e2)[g % 2][:, :, :], acc[:, g * GROUP:(g + 1) * GROUP, :],
                                   ACT.Square).then_inc(ln_squared, 1)
                act.wait_ge(ln_mm, 2 * n + 2)
                act.activation(ln_std, ps[:, 1, 0:T], ACT.Sqrt, bias=eps[:, 0:1]).then_inc(ln_root, 1)
                for g in range(NG):
                    rows = slice(g * GROUP, (g + 1) * GROUP)
                    e = f1[:, :].rearrange("p (c t) -> p c t", t=T)[:, rows, :] if last else (e1, e2)[g % 2][:, :, :]
                    act.wait_ge(ln_scaled, n * NG + g + 1)
                    for k in range(GROUP):
                        c = n * NC + g * GROUP + k
                        v = act.activation(e[:, k, :], acc[:, g * GROUP + k, :] , ACT.Identity,
                                           scale=prm[:, C_LNG + c:C_LNG + c + 1],
                                           bias=prm[:, C_LNB + c:C_LNB + c + 1])
                    v.then_inc(ln_value, 1)
                    if not last:
                        act.wait_ge(ln_value, n * NG + g + 1)
                        act.activation(xin[:, rows, 0, :], e, ACT.Copy).then_inc(ln_hi, 1)
                        if g >= 1 and g + 1 < NG:
                            act.wait_ge(pair_ready, (R_LN0, R_LN1, R_LN2)[n] + g)

            def mlp(b0, sq, end=False):
                def w1_turns(s, h):
                    for j in range(2):
                        b = b0 + s * SLAB_BLOCKS + h * (2 * BLOCKS) + j * BLOCKS
                        m = sq + s * NG + h * 2 + j
                        splits(b, b0 // BLOCKS + s * (2 * NG) + h * 2 + j)
                        take_hl(j, b, e1[:, :, :], sq_hl)
                        act.wait_ge(sq_val, m + 1)
                        rows = bass.ds(h * (2 * GROUP) + j * GROUP, GROUP)
                        act.activation(hid[:, rows, 0, :], e2[:, :, :], ACT.Copy).then_inc(sq_hi, 1)

                def w2_turns(s, h, last=False):
                    for j in range(2):
                        b = b0 + NG * BLOCKS + s * SLAB_BLOCKS + h * (2 * BLOCKS) + j * BLOCKS
                        splits(b, b0 // BLOCKS + NG + s * (2 * NG) + h * 2 + j, AHEAD,
                               BLOCKS if last and j else AHEAD + BLOCKS)

                with act.Fori(0, SLABS - 1) as s:
                    with act.Fori(0, NG // 2) as h:
                        w1_turns(s, h)
                    with act.Fori(0, NG // 2) as h:
                        w2_turns(s, h)
                with act.Fori(0, NG // 2) as h:
                    w1_turns(SLABS - 1, h)
                w2_turns(SLABS - 1, 0)
                w2_turns(SLABS - 1, 1, end)

            plain_unit(B_RO)
            layer_norm()
            mlp(B_MLP0, 0)
            layer_norm()
            with act.Fori(0, NG // 2) as it:
                for j in range(2):
                    g = it * 2 + j
                    b = B_QKV + it * (6 * BLOCKS) + j * (3 * BLOCKS)
                    no = B_QKV // BLOCKS + it * 6 + j * 3
                    for part, dst in enumerate((qg, kg)):
                        splits(b + part * BLOCKS, no + part)
                        take_hl((j, 1 - j)[part], b + part * BLOCKS, dst, hl_copied)
                    bv, nv = b + 2 * BLOCKS, no + 2
                    splits(bv, nv, AHEAD, AHEAD + 5)
                    act.wait_ge(bias_ready, g + 1)
                    for h in range(GROUP):
                        for a, cols in enumerate((slice(0, P), slice(P, 3 * P))):
                            ex = act.activation(prob[:, h, cols], prob[:, h, cols], ACT.Exp, scale=QK_SCALE,
                                                bias=stat[:, h, 2 + a:3 + a], accum_out=stat[:, h, 4 + a:5 + a])
                    ex.then_inc(exp_done, 1)
                    splits(bv, nv, AHEAD + 5)
                    act.wait_ge(mm_done, bv + BLOCKS)
                    act.activation(vg, banks(j)[:, 0:2, :], ACT.Copy).then_inc(v_stored, 1)
                    for h in range(GROUP):
                        act.wait_ge(pt_done, it * (2 * GROUP) + j * GROUP + h + 1)
                        act.activation(probt[:, h, :], banks(1 - j)[:, h, 0:3 * P], ACT.Copy)\
                           .then_inc(pt_copied, 1)
                    act.wait_ge(pv_done, g + 1)
                    act.activation(hid[:, bass.ds(g * GROUP, GROUP), 0, :],
                                   banks(j)[:, 2:4, :].rearrange("p b (c t) -> p (b c) t", t=T),
                                   ACT.Copy).then_inc(pv_hi, 1)
            plain_unit(B_MO)
            layer_norm()
            mlp(B_MLP1, SLABS * NG, end=True)
            layer_norm(last=True)

        @block.vector
        def _(dve):
            def split_lo(b, off):
                dve.wait_ge(wh_done, b + (off + 1))
                if not (isinstance(b, int) and b + off < SPLITS):
                    dve.wait_ge(mm_done, b + (off - (SPLITS - 1)))
                dve.tensor_tensor(wl[:, off % SPLITS, :], wst[:, off % BLOCKS, :], wh[:, off % SPLITS, :],
                                  ALU.subtract).then_inc(wl_done, 1)

            def splits(b, lo=AHEAD, hi=AHEAD + BLOCKS):
                for off in range(lo, hi):
                    split_lo(b, off)

            def add_hh(half, dst, copied, n):
                dve.wait_ge(copied, n)
                return dve.tensor_tensor(dst, dst, banks(half)[:, :, 0:T], ALU.add)

            for g in range(NG):
                dve.wait_ge(xt_hi, g + 1)
                rows = slice(g * GROUP, (g + 1) * GROUP)
                dve.tensor_tensor(xin[:, rows, 1, :],
                                  ps[:, 2 * g:2 * g + 2, :].rearrange("p b (c t) -> p (b c) t", t=T),
                                  xin[:, rows, 0, :], ALU.subtract).then_inc(pair_ready, 1)
                if g == 1:
                    dve.wait_ge(pair_ready, 2)
                    dve.sem_inc(psum_free, 1)
            dve.wait_ge(pair_ready, NG)
            dve.sem_inc(psum_free, 1)
            dve.wait_ge(prm_t, 1)
            dve.tensor_copy(prm[:, :], ps[:, 0, 0:256]).then_inc(prm_ready, 1)
            dve.wait_ge(prm_ready, 1)

            links = [0]

            def link(ins):
                links[0] += 1
                ins.then_inc(sp_link, 1)
                dve.wait_ge(sp_link, links[0])

            lam = prm[:, C_LAM:C_LAM + NC]
            absl, y, den, s, z, p, neg8, pos8 = (small[:, k, :] for k in range(8))
            link(dve.tensor_scalar(den, lam, -1.0, None, ALU.mult))
            dve.tensor_tensor(absl, lam, den, ALU.max).then_inc(sp_abs, 1)
            dve.wait_ge(sp_exp, 1)
            link(dve.tensor_scalar(den, y, 2.0, None, ALU.add))
            link(dve.reciprocal(den, den))
            link(dve.tensor_tensor(s, y, den, ALU.mult))
            link(dve.tensor_tensor(z, s, s, ALU.mult))
            link(dve.tensor_scalar(p, z, 1.0 / 17, None, ALU.mult))
            for k in range(15, 1, -2):
                link(dve.scalar_tensor_tensor(out=p, in0=p, scalar=1.0 / k, in1=z, op0=ALU.add, op1=ALU.mult))
            link(dve.scalar_tensor_tensor(out=p, in0=p, scalar=1.0, in1=s, op0=ALU.add, op1=ALU.mult))
            link(dve.tensor_scalar(den, lam, -1.0, 0.0, ALU.mult, ALU.max))
            link(dve.scalar_tensor_tensor(out=p, in0=p, scalar=2.0, in1=den, op0=ALU.mult, op1=ALU.add))
            link(dve.tensor_scalar(neg8, p, -LRU_C, None, ALU.mult))
            dve.tensor_scalar(pos8, p, LRU_C, None, ALU.mult).then_inc(sp_ready, 1)

            splits(0, 0, AHEAD)
            for t in range(NG):
                b = B_U + t * BLOCKS
                rows = slice(t * GROUP, (t + 1) * GROUP)
                splits(b)
                add_hh(t % 2, u3[:, rows, :], hl_copied, t + 1).then_inc(psum_free, 1)
                dve.wait_ge(psum_free, 2 + T_U + t + 1)
                if t >= 1:
                    dve.wait_ge(conv_hi, t)
                for k in range(CONV):
                    shift = k
                    for q in range(GROUP):
                        c = t * GROUP + q
                        col = C_CONVW + (CONV - 1 - k) * NC + c
                        if k == 0:
                            ins = dve.tensor_scalar(e1[:, q, :], u3[:, c, :], prm[:, col:col + 1],
                                                    prm[:, C_CONVB + c:C_CONVB + c + 1], ALU.mult, ALU.add)
                        else:
                            ins = dve.scalar_tensor_tensor(out=e1[:, q, shift:T], in0=u3[:, c, 0:T - shift],
                                                           scalar=prm[:, col:col + 1], in1=e1[:, q, shift:T],
                                                           op0=ALU.mult, op1=ALU.add)
                    ins.then_inc(conv_link, 1)
                    dve.wait_ge(conv_link, t * CONV + k + 1)
                dve.wait_ge(conv_hi, t + 1)
                dve.tensor_tensor(hid[:, rows, 1, :], e1[:, :, :], hid[:, rows, 0, :], ALU.subtract)\
                   .then_inc(pair_ready, 1)
            splits(B_GATES)

            rl = [0]

            def rlink(ins):
                rl[0] += 1
                ins.then_inc(rec_link, 1)
                dve.wait_ge(rec_link, rl[0])

            dve.wait_ge(sig_done, 4)
            for t in range(NG):
                b = B_G + t * BLOCKS
                rows = slice(t * GROUP, (t + 1) * GROUP)
                splits(b, AHEAD, AHEAD + 1)
                dve.wait_ge(at_done, t + 1)
                rlink(dve.tensor_scalar(e1[:, :, :], r3[:, rows, :], 1.0, None, ALU.add))
                rlink(dve.reciprocal(e1[:, :, :], e1[:, :, :]))
                dve.tensor_tensor(e1[:, :, :], e1[:, :, :], r3[:, rows, :], ALU.mult).then_inc(rec_ratio, 1)
                splits(b, AHEAD + 1, AHEAD + 4)
                rlink(dve.tensor_tensor(e2[:, :, :], hid[:, rows, 0, :], hid[:, rows, 1, :], ALU.add))
                rlink(dve.tensor_tensor(e2[:, :, :], e2[:, :, :], i3[:, rows, :], ALU.mult))
                dve.wait_ge(rec_root, t + 1)
                rlink(dve.tensor_tensor(e2[:, :, :], e2[:, :, :], e1[:, :, :], ALU.mult))
                splits(b, AHEAD + 4, AHEAD + 6)
                for q in range(GROUP):
                    c = t * GROUP + q
                    ins = dve.tensor_tensor_scan(out=i3[:, c, :], data0=u3[:, c, :], data1=e2[:, q, :],
                                                 initial=0.0, op0=ALU.mult, op1=ALU.add)
                ins.then_inc(h_ready, 1)
                dve.wait_ge(h_ready, t + 1)
                splits(b, AHEAD + 6)
                add_hh(t % 2, acc[:, rows, :], hl_copied, T_G + t + 1).then_inc(psum_free, 1)
            for g in range(NG):
                rows = slice(g * GROUP, (g + 1) * GROUP)
                e = (e1, e2)[g % 2]
                dve.wait_ge(gelu_done, g + 1)
                dve.tensor_tensor(e[:, :, :], acc[:, rows, :], i3[:, rows, :], ALU.mult).then_inc(prod_done, 1)
                dve.wait_ge(prod_hi, g + 1)
                dve.tensor_tensor(hid[:, rows, 1, :], e[:, :, :], hid[:, rows, 0, :], ALU.subtract)\
                   .then_inc(pair_ready, 1)

            def add_turn(half, b, rows, n):
                dve.wait_ge(mm_done, b + BLOCKS)
                dve.tensor_tensor(acc[:, rows, :], acc[:, rows, :], banks(half)[:, :, 0:T], ALU.add)\
                   .then_inc(acc_half, 1)
                dve.wait_ge(acc_half, n + 1)
                dve.tensor_tensor(acc[:, rows, :], acc[:, rows, :], banks(half)[:, :, T:2 * T], ALU.add)\
                   .then_inc(psum_free, 1)

            def out_unit(b0, use, n0):
                with dve.Fori(0, NG // 2) as h:
                    for j in range(2):
                        b = b0 + h * (2 * BLOCKS) + j * BLOCKS
                        splits(b)
                        dve.wait_ge(acc_ready, NG * use + NG)
                        add_turn(j, b, bass.ds(h * (2 * GROUP) + j * GROUP, GROUP), n0 + h * 2 + j)

            n_ln = [0]

            def layer_norm(turns_freed, last=False):
                n = n_ln[0]
                n_ln[0] += 1
                dve.wait_ge(psum_free, 2 + turns_freed)
                dve.tensor_reduce(ln_sum, acc[:, :, :].rearrange("p c t -> p t c"), AX_X, ALU.add)\
                   .then_inc(ln_stepd, 1)
                dve.wait_ge(ln_mm, 2 * n + 1)
                dve.tensor_copy(ln_mean, ps[:, 0, 0:T]).then_inc(ln_stepd, 1)
                dve.wait_ge(ln_stepd, 3 * n + 2)
                for g in range(NG):
                    rows = slice(g * GROUP, (g + 1) * GROUP)
                    dve.tensor_tensor(acc[:, rows, :], acc[:, rows, :],
                                      ln_mean.unsqueeze(1).to_broadcast([P, GROUP, T]), ALU.subtract)\
                       .then_inc(ln_centred, 1)
                for g in range(NG):
                    dve.wait_ge(ln_squared, n * NG + g + 1)
                    dve.tensor_reduce(ln_sq[:, g, :], (e1, e2)[g % 2][:, :, :].rearrange("p c t -> p t c"),
                                      AX_X, ALU.add).then_inc(ln_reduced, 1)
                dve.wait_ge(ln_root, n + 1)
                dve.reciprocal(ln_rstd, ln_std).then_inc(ln_stepd, 1)
                dve.wait_ge(ln_stepd, 3 * n + 3)
                for g in range(NG):
                    rows = slice(g * GROUP, (g + 1) * GROUP)
                    dve.tensor_tensor(acc[:, rows, :], acc[:, rows, :],
                                      ln_rstd.unsqueeze(1).to_broadcast([P, GROUP, T]), ALU.mult)\
                       .then_inc(ln_scaled, 1)
                    if g >= 1 and not last:
                        ln_lo(n, g - 1)
                if not last:
                    ln_lo(n, NG - 1)

            def ln_lo(n, g):
                rows = slice(g * GROUP, (g + 1) * GROUP)
                dve.wait_ge(ln_hi, n * NG + g + 1)
                dve.tensor_tensor(xin[:, rows, 1, :], (e1, e2)[g % 2][:, :, :], xin[:, rows, 0, :],
                                  ALU.subtract).then_inc(pair_ready, 1)

            def mlp(b0, sq, use, n0, free, end=False):
                def w1_turns(s, h):
                    for j in range(2):
                        b = b0 + s * SLAB_BLOCKS + h * (2 * BLOCKS) + j * BLOCKS
                        m = sq + s * NG + h * 2 + j
                        rows = bass.ds(h * (2 * GROUP) + j * GROUP, GROUP)
                        splits(b, AHEAD, AHEAD + BLOCKS - 1)
                        add_hh(j, e1[:, :, :], sq_hl, m + 1).then_inc(psum_free, 1)
                        dve.wait_ge(psum_free, 2 + free + s * (2 * NG) + h * 2 + (j + 1))
                        dve.scalar_tensor_tensor(out=e2[:, :, :], in0=e1[:, :, :], scalar=0.0, in1=e1[:, :, :],
                                                 op0=ALU.max, op1=ALU.mult).then_inc(sq_val, 1)
                        splits(b, AHEAD + BLOCKS - 1)
                        dve.wait_ge(sq_hi, m + 1)
                        dve.tensor_tensor(hid[:, rows, 1, :], e2[:, :, :], hid[:, rows, 0, :], ALU.subtract)\
                           .then_inc(pair_ready, 1)

                def w2_turns(s, h, last=False):
                    for j in range(2):
                        b = b0 + NG * BLOCKS + s * SLAB_BLOCKS + h * (2 * BLOCKS) + j * BLOCKS
                        splits(b, AHEAD, BLOCKS if last and j else AHEAD + BLOCKS)
                        dve.wait_ge(acc_ready, NG * use + NG)
                        add_turn(j, b, bass.ds(h * (2 * GROUP) + j * GROUP, GROUP),
                                 n0 + s * NG + h * 2 + j)

                with dve.Fori(0, SLABS - 1) as s:
                    with dve.Fori(0, NG // 2) as h:
                        w1_turns(s, h)
                    with dve.Fori(0, NG // 2) as h:
                        w2_turns(s, h)
                with dve.Fori(0, NG // 2) as h:
                    w1_turns(SLABS - 1, h)
                w2_turns(SLABS - 1, 0)
                w2_turns(SLABS - 1, 1, end)

            out_unit(B_RO, 0, 0)
            layer_norm(T_RO + NG)
            mlp(B_MLP0, 0, 1, NG, T_MLP0)
            layer_norm(T_MLP0 + 2 * SLABS * NG)

            cos_t = ropet[:, 0:1, :].to_broadcast([32, GROUP, T])
            sin_t = ropet[:, 1:2, :].to_broadcast([32, GROUP, T])
            swap = [k ^ ROPE_HALF for k in range(32)]
            dve.wait_ge(consts, 7)
            with dve.Fori(0, NG // 2) as it:
                for j in range(2):
                    g = it * 2 + j
                    b = B_QKV + it * (6 * BLOCKS) + j * (3 * BLOCKS)
                    for part, dst in enumerate((qg, kg)):
                        splits(b + part * BLOCKS)
                        links = it * 12 + 6 * j + 3 * part
                        n = it * 4 + 2 * j + part
                        add_hh((j, 1 - j)[part], dst, hl_copied, T_RO + n + 1).then_inc(qk_link, 1)
                        dve.wait_ge(qk_link, links + 1)
                        dve.tensor_tensor(cosd[0:32, :, :], dst[0:32, :, :], cos_t, ALU.mult)
                        dve.stream_shuffle(rot[0:32, :, :], dst[0:32, :, :], swap).then_inc(qk_link, 1)
                        dve.wait_ge(qk_link, links + 2)
                        dve.tensor_tensor(rot[0:32, :, :], rot[0:32, :, :], sin_t, ALU.mult)\
                           .then_inc(qk_link, 1)
                        dve.wait_ge(qk_link, links + 3)
                        dve.tensor_tensor(dst[0:32, :, :], cosd[0:32, :, :], rot[0:32, :, :], ALU.add)\
                           .then_inc(qk_ready, 1)
                    bv = b + 2 * BLOCKS
                    al = it * 6 + 3 * j
                    splits(bv, AHEAD, AHEAD + 3)
                    dve.wait_ge(scores_done, g + 1)
                    dve.tensor_tensor(prob, banks(1 - j)[:, :, 0:3 * P],
                                      maskt[:, :].unsqueeze(1).to_broadcast([P, GROUP, 3 * P]), ALU.add)\
                       .then_inc(att_link, 1)
                    dve.wait_ge(att_link, al + 1)
                    dve.tensor_reduce(stat[:, :, 0:1], prob[:, :, 0:P], AX_X, ALU.max)
                    dve.tensor_reduce(stat[:, :, 1:2], prob[:, :, P:3 * P], AX_X, ALU.max)\
                       .then_inc(att_link, 1)
                    dve.wait_ge(att_link, al + 2)
                    dve.tensor_scalar(stat[:, :, 2:4], stat[:, :, 0:2], -QK_SCALE, None, ALU.mult)\
                       .then_inc(bias_ready, 1)
                    splits(bv, AHEAD + 3, AHEAD + 5)
                    dve.wait_ge(exp_done, g + 1)
                    dve.reciprocal(stat[:, :, 6:8], stat[:, :, 4:6]).then_inc(att_link, 1)
                    dve.wait_ge(att_link, al + 3)
                    dve.tensor_tensor(prob[:, :, 0:P], prob[:, :, 0:P],
                                      stat[:, :, 6:7].to_broadcast([P, GROUP, P]), ALU.mult)
                    dve.tensor_tensor(prob[:, :, P:3 * P], prob[:, :, P:3 * P],
                                      stat[:, :, 7:8].to_broadcast([P, GROUP, 2 * P]), ALU.mult)\
                       .then_inc(p_ready, 1)
                    splits(bv, AHEAD + 5)
                    dve.wait_ge(pv_hi, g + 1)
                    rows = bass.ds(g * GROUP, GROUP)
                    dve.tensor_tensor(hid[:, rows, 1, :],
                                      banks(j)[:, 2:4, :].rearrange("p b (c t) -> p (b c) t", t=T),
                                      hid[:, rows, 0, :], ALU.subtract).then_inc(pair_ready, 1)
            out_unit(B_MO, 2, NG + SLABS * NG)
            layer_norm(T_MO + NG)
            mlp(B_MLP1, SLABS * NG, 3, 2 * NG + SLABS * NG, T_MLP1, end=True)
            layer_norm(T_MLP1 + 2 * SLABS * NG, last=True)
            o3 = f2[:, :].rearrange("p (a n) -> p a n", a=HALVES)
            for g in range(NG):
                dve.wait_ge(out_t, g + 1)
                dve.tensor_copy(o3[:, :, g * COLS:(g + 1) * COLS],
                                banks(1)[:, 2 * (g % 2):2 * (g % 2) + 2, :]).then_inc(out_copied, 1)


_INS = ["x", "ln_g", "ln_b", "mlp_w1", "mlp_w2", "rg_w_in", "rg_conv_w", "rg_conv_b", "rg_gate_a_w",
        "rg_gate_a_b", "rg_gate_x_w", "rg_gate_x_b", "rg_lambda", "rg_w_out", "moba_w_qkv", "moba_w_out"]


def rope_table():
    inv = np.float32(500000.0) ** (-np.arange(0, 32, 2, dtype=np.float32) / np.float32(32))
    ang = np.arange(T, dtype=np.float32)[None, :] * inv.astype(np.float32)[:, None]
    cos, sin = np.cos(ang).astype(np.float32), np.sin(ang).astype(np.float32)
    return np.stack([np.concatenate([cos, cos]), np.concatenate([-sin, sin])], axis=1)


def kernel(**inputs):
    import concourse.bacc as _bacc
    from concourse.bass_utils import run_bass_kernel_spmd as _run

    nc = _bacc.Bacc("TRN2", target_bir_lowering=False, num_devices=1)
    arrays, args = {}, []
    given = {n: inputs[n] for n in _INS}
    given["rope"] = rope_table()
    for name, value in given.items():
        a = np.ascontiguousarray(value)
        arrays[f"in_{name}_dram"] = a
        args.append(nc.dram_tensor(f"in_{name}_dram", a.shape, mybir.dt.from_np(a.dtype),
                                   kind="ExternalInput").ap())
    out = nc.dram_tensor("out_dram", (1, T, D), F32, kind="ExternalOutput").ap()
    build_trunk(nc, *args, out)
    r = _run(nc, [arrays], core_ids=[0])
    return r.results[0]["out_dram"]
```

```python
from contextlib import ExitStack

import numpy as np

import concourse.bass as bass
from concourse import mybir

F32 = mybir.dt.float32
F32R = mybir.dt.float32r
ALU = mybir.AluOpType
ACT = mybir.ActivationFunctionType
AX_X = mybir.AxisListType.X

P = 128
T = 256
D = 2048
NC = D // P
HALVES = T // P
GROUP = 4
NG = NC // GROUP
COLS = GROUP * P
KCH = 2
BLOCKS = NC // KCH
BLK = KCH * COLS
SPLITS = 4
AHEAD = 4
D_FF = 8192
SLABS = D_FF // D
LRU_BLOCKS = 8
LRU_W = D // LRU_BLOCKS
CONV = 4
LRU_C = 8.0
ROPE_HALF = 16
DEPTH = 2
ALPHA = (2.0 * DEPTH) ** 0.25
LN_EPS = 1e-5
QK_SCALE = 128 ** -0.5
NEG = -1e30

B_U = 0
B_GATES = B_U + NG * BLOCKS
B_G = B_GATES + BLOCKS
B_RO = B_G + NG * BLOCKS
B_MLP0 = B_RO + NG * BLOCKS
B_QKV = B_MLP0 + 2 * SLABS * NG * BLOCKS
B_MO = B_QKV + 3 * NG * BLOCKS
B_MLP1 = B_MO + NG * BLOCKS
B_END = B_MLP1 + 2 * SLABS * NG * BLOCKS
SLAB_BLOCKS = 2 * NG * BLOCKS

T_U, T_G, T_RO, T_MLP0, T_MO, T_MLP1 = 0, 4, 8, 12, 44, 48

R_X, R_CONV, R_RO, R_LN0, R_SQ0, R_LN1, R_ATT, R_LN2, R_SQ1 = 0, 8, 16, 24, 32, 64, 72, 80, 88
AHEAD_X = 3
LATE = AHEAD + BLOCKS - 1
START = AHEAD + 2
NEXT = LATE + 3
STEPS = NC // 2
DVE_STEPS = 1
PIECES = ((0, 2), (2, 3), (3, 4))

C_LNG, C_LNB, C_CONVW, C_CONVB, C_BA, C_BX, C_LAM = 0, 64, 128, 192, 208, 224, 240


def build_trunk(nc, x, ln_g, ln_b, mlp_w1, mlp_w2, rg_w_in, rg_conv_w, rg_conv_b, rg_gate_a_w,
                rg_gate_a_b, rg_gate_x_w, rg_gate_x_b, rg_lambda, rg_w_out, moba_w_qkv, moba_w_out,
                rope, out):
    with ExitStack() as ctx:
        def sb(name, shape, dt=F32):
            return ctx.enter_context(nc.sbuf_tensor(name, shape, dt))

        def sem(name):
            return ctx.enter_context(nc.semaphore(name))

        xin = sb("xin", [P, NC, 2, T], F32R)
        hid = sb("hid", [P, NC, 2, T], F32R)
        acc = sb("acc", [P, NC, T])
        f1 = sb("f1", [P, NC * T])
        f2 = sb("f2", [P, NC * T])
        f3 = sb("f3", [P, NC * T])
        e1 = sb("e1", [P, GROUP, T])
        e2 = sb("e2", [P, GROUP, T])
        wst = sb("wst", [P, BLOCKS, BLK])
        wh = sb("wh", [P, SPLITS, BLK], F32R)
        wl = sb("wl", [P, SPLITS, BLK], F32R)
        prm = sb("prm", [P, 256])
        ident = sb("ident", [P, P])
        eps = sb("eps", [P, 1])
        ones = sb("ones", [P, P])
        maskt = sb("maskt", [P, 3 * P])
        ropet = sb("ropet", [32, 2, T])
        small = sb("small", [P, 8, NC])
        stat = sb("stat", [P, 4, 8])
        ps = ctx.enter_context(nc.psum_tensor("ps", [P, 8, 512], F32))

        u3 = f1[:, :].rearrange("p (c t) -> p c t", t=T)
        r3 = f2[:, :].rearrange("p (c t) -> p c t", t=T)
        i3 = f3[:, :].rearrange("p (c t) -> p c t", t=T)
        qg = f1[:, 0:1024].rearrange("p (c t) -> p c t", t=T)
        kg = f1[:, 1024:2048].rearrange("p (c t) -> p c t", t=T)
        vg = f1[:, 2048:3072].rearrange("p (a n) -> p a n", a=HALVES)
        rot = f1[:, 3072:4096].rearrange("p (c t) -> p c t", t=T)
        cosd = f2[:, 3072:4096].rearrange("p (c t) -> p c t", t=T)
        prob = f2[:, 0:1536].rearrange("p (h n) -> p h n", n=3 * P)
        probt = f2[:, 1536:3072].rearrange("p (h n) -> p h n", n=3 * P)
        (ln_shift, ln_sum, ln_sumsq, ln_pair, ln_pairsq, ln_mean, ln_sqm, ln_var_t, ln_std, ln_rstd) = \
            (f3[:, k * T:(k + 1) * T] for k in range(10))
        squares = f1[:, :].rearrange("p (c t) -> p c t", t=T)

        stage_full = [sem(f"stage_full{s}") for s in range(BLOCKS)]
        x_loaded = [sem(f"x_loaded{k}") for k in range(BLOCKS)]
        prm_loaded = sem("prm_loaded")
        wh_done = sem("wh_done")
        wl_done = sem("wl_done")
        mm_done = sem("mm_done")
        pair_ready = sem("pair_ready")
        psum_free = sem("psum_free")
        xt_done = sem("xt_done")
        xt_hi = sem("xt_hi")
        eps_ready = sem("eps_ready")
        consts = sem("consts")
        prm_t = sem("prm_t")
        prm_ready = sem("prm_ready")
        sp_link = sem("sp_link")
        sp_abs = sem("sp_abs")
        sp_exp = sem("sp_exp")
        sp_ready = sem("sp_ready")
        hl_copied = sem("hl_copied")
        conv_begun = sem("conv_begun")
        conv_link = sem("conv_link")
        conv_hi = sem("conv_hi")
        sig_done = sem("sig_done")
        ui_sum = sem("ui_sum")
        b_ready = sem("b_ready")
        ui_ready = sem("ui_ready")
        tanh_done = sem("tanh_done")
        rec_root = sem("rec_root")
        rec_link = sem("rec_link")
        h_ready = sem("h_ready")
        gelu_done = sem("gelu_done")
        prod_done = sem("prod_done")
        prod_hi = sem("prod_hi")
        acc_half = sem("acc_half")
        pool_sum = sem("pool_sum")
        acc_ready = sem("acc_ready")
        sq_hl = sem("sq_hl")
        sq_val = sem("sq_val")
        sq_hi = sem("sq_hi")
        ln_part = sem("ln_part")
        ln_mm = sem("ln_mm")
        ln_shifted = sem("ln_shifted")
        ln_centred = sem("ln_centred")
        ln_late = sem("ln_late")
        ln_squared = sem("ln_squared")
        ln_sums = sem("ln_sums")
        piece_mm = sem("piece_mm")
        piece_half = sem("piece_half")
        piece_added = sem("piece_added")
        ln_pairs = sem("ln_pairs")
        ln_sqmean = sem("ln_sqmean")
        ln_copied = sem("ln_copied")
        ln_var = sem("ln_var")
        ln_root = sem("ln_root")
        ln_inv = sem("ln_inv")
        ln_zero = sem("ln_zero")
        ln_zero_p = sem("ln_zero_p")
        ln_scaled = sem("ln_scaled")
        ln_hi = sem("ln_hi")
        qk_link = sem("qk_link")
        qk_ready = sem("qk_ready")
        scores_done = sem("scores_done")
        att_link = sem("att_link")
        bias_ready = sem("bias_ready")
        exp_done = sem("exp_done")
        p_ready = sem("p_ready")
        v_stored = sem("v_stored")
        pt_done = sem("pt_done")
        pt_copied = sem("pt_copied")
        pv_done = sem("pv_done")
        pv_hi = sem("pv_hi")
        out_t = sem("out_t")
        out_copied = sem("out_copied")
        stored = sem("stored")

        def banks(half):
            return ps[:, 4 * half:4 * half + 4, :]

        def xt_bank(k):
            return ps[:, 4 + k % 4, :].rearrange("p (c t) -> p c t", t=T)

        def cols_of(w, first):
            return w.rearrange("(b k p) n -> b p k n", k=KCH, p=P)[:, :, :, bass.ds(first, COLS)]

        block = ctx.enter_context(nc.Block())

        @block.sync
        def _(sp):
            def load_block(src, kb, b):
                if b is not None:
                    sp.wait_ge(wl_done, b - (BLOCKS - 1))
                sp.dma_start(wst[:, kb, :].rearrange("p (k n) -> p k n", k=KCH), src)\
                  .then_inc(stage_full[kb], 16)

            def load_turn(w, col, b):
                col = sp.snap(col)
                src = cols_of(w, col)
                for kb in range(BLOCKS):
                    load_block(src[kb], kb, b + kb)

            w_in = rg_w_in[0]
            first = cols_of(w_in, D)
            x_tok = f1[:, :].rearrange("p (a n) -> p a n", a=HALVES)
            x_src = x[0].rearrange("(a p) n -> p a n", p=P)
            for kb in range(BLOCKS):
                pair = slice(kb * KCH * P, (kb + 1) * KCH * P)
                sp.dma_start(x_tok[:, :, pair], x_src[:, :, pair]).then_inc(x_loaded[kb], 16)
                load_block(first[kb], kb, None)
            for dst, src in ((f2[0:64, 0:P], ln_g.rearrange("a b (c p) -> (a b c) p", p=P)),
                             (f2[64:128, 0:P], ln_b.rearrange("a b (c p) -> (a b c) p", p=P)),
                             (f2[0:64, P:2 * P], rg_conv_w.rearrange("l k (c p) -> (l k c) p", p=P)),
                             (f2[64:80, P:2 * P], rg_conv_b.rearrange("l (c p) -> (l c) p", p=P)),
                             (f2[80:96, P:2 * P], rg_gate_a_b.rearrange("l n (c p) -> (l n c) p", p=P)),
                             (f2[96:112, P:2 * P], rg_gate_x_b.rearrange("l n (c p) -> (l n c) p", p=P)),
                             (f2[112:128, P:2 * P], rg_lambda.rearrange("l (c p) -> (l c) p", p=P)),
                             (ropet[:, :, :], rope)):
                sp.dma_start(dst, src).then_inc(prm_loaded, 16)
            with sp.Fori(1, NG) as t:
                load_turn(w_in, D + t * COLS, B_U + t * BLOCKS)
            for gb in range(BLOCKS):
                w = (rg_gate_a_w, rg_gate_x_w)[(gb // 2) % 2]
                n0 = (gb // 4) * 4 + (gb % 2) * 2
                sp.wait_ge(wl_done, B_GATES + gb - (BLOCKS - 1))
                sp.dma_start(wst[:, gb, :].rearrange("p (k n) -> p k n", n=LRU_W),
                             w[0, n0:n0 + 2].rearrange("n (k p) v -> p (n k) v", p=P))\
                  .then_inc(stage_full[gb], 16)
            with sp.Fori(0, NG) as t:
                load_turn(w_in, t * COLS, B_G + t * BLOCKS)
            with sp.Fori(0, NG) as t:
                load_turn(rg_w_out[0], t * COLS, B_RO + t * BLOCKS)

            def load_mlp(layer, b0):
                with sp.Fori(0, SLABS) as s:
                    with sp.Fori(0, NG) as t:
                        load_turn(mlp_w1[layer], s * D + t * COLS,
                                  b0 + s * SLAB_BLOCKS + t * BLOCKS)
                    w2 = mlp_w2[layer].rearrange("(s r) n -> s r n", r=D)
                    with sp.Fori(0, NG) as t:
                        b = b0 + NG * BLOCKS + s * SLAB_BLOCKS + t * BLOCKS
                        slab = sp.snap(s + 0)
                        col = sp.snap(t * COLS)
                        for kb in range(BLOCKS):
                            src = w2[bass.ds(slab, 1), kb * KCH * P:(kb + 1) * KCH * P,
                                     bass.ds(col, COLS)]
                            load_block(src.rearrange("s (k p) n -> p (s k) n", p=P), kb, b + kb)

            load_mlp(0, B_MLP0)
            with sp.Fori(0, NG) as g:
                for part in range(3):
                    load_turn(moba_w_qkv[0], part * D + g * COLS,
                              B_QKV + (3 * g + part) * BLOCKS)
            with sp.Fori(0, NG) as t:
                load_turn(moba_w_out[0], t * COLS, B_MO + t * BLOCKS)
            load_mlp(1, B_MLP1)
            o3 = f2[:, :].rearrange("p (a n) -> p a n", a=HALVES)
            for g in range(NG):
                sp.wait_ge(out_copied, g + 1)
                sp.dma_start(out[0].rearrange("(a p) n -> p a n", p=P)[:, :, g * COLS:(g + 1) * COLS],
                             o3[:, :, g * COLS:(g + 1) * COLS]).then_inc(stored, 16)
            sp.wait_ge(stored, 16 * NG)

        @block.gpsimd
        def _(pool):
            pool.memset(ident[:, :], 0.0).then_inc(consts, 1)
            pool.memset(ones[:, :], 1.0 / D).then_inc(consts, 1)
            pool.memset(maskt[:, :], 0.0).then_inc(consts, 1)
            pool.wait_ge(consts, 3)
            pool.affine_select(out=ident[:, :], in_=ident[:, :], compare_op=ALU.not_equal, fill=1.0,
                               base=0, pattern=[[-1, P]], channel_multiplier=1).then_inc(consts, 1)
            for lo, base, n in ((0, 0, P), (P, P, 2 * P)):
                pool.affine_select(out=maskt[:, lo:lo + n], in_=maskt[:, lo:lo + n],
                                   compare_op=ALU.is_ge, fill=NEG, base=base,
                                   pattern=[[-1, n]], channel_multiplier=1).then_inc(consts, 1)

            pool.wait_ge(sig_done, 4)
            for g in range(NG):
                rows = slice(g * GROUP, (g + 1) * GROUP)
                if g >= 1:
                    pool.wait_ge(ui_ready, g)
                pool.tensor_tensor(e1[:, :, :], hid[:, rows, 0, :], hid[:, rows, 1, :], ALU.add)\
                    .then_inc(ui_sum, 1)
                pool.wait_ge(ui_sum, g + 1)
                pool.tensor_tensor(i3[:, rows, :], i3[:, rows, :], e1[:, :, :], ALU.mult)\
                    .then_inc(ui_ready, 1)

            for g in range(NG):
                rows = slice(g * GROUP, (g + 1) * GROUP)
                pool.wait_ge(rec_link, g + 1)
                pool.wait_ge(ui_ready, g + 1)
                pool.tensor_tensor(i3[:, rows, :], i3[:, rows, :], r3[:, rows, :], ALU.mult)\
                    .then_inc(b_ready, 1)

            def residual(use, ready):
                for g in range(NG):
                    rows = slice(g * GROUP, (g + 1) * GROUP)
                    pool.wait_ge(pair_ready, ready + 2 * g + 2)
                    pool.tensor_tensor(acc[:, rows, :], xin[:, rows, 0, :], xin[:, rows, 1, :],
                                       ALU.add).then_inc(pool_sum, 1)
                    pool.wait_ge(pool_sum, use * NG + g + 1)
                    pool.tensor_scalar(acc[:, rows, :], acc[:, rows, :], ALPHA, None, ALU.mult)\
                        .then_inc(acc_ready, 1)

            def norm(n):
                pool.wait_ge(piece_added, 2 * n + 1)
                pool.tensor_tensor(ln_pair, acc[:, 12, :], acc[:, 13, :], ALU.add).then_inc(ln_pairs, 1)
                pool.wait_ge(ln_squared, 6 * n + 4)
                pool.tensor_tensor(ln_pairsq, squares[:, 12, :], squares[:, 13, :], ALU.add)\
                    .then_inc(ln_pairs, 1)
                pool.wait_ge(ln_copied, n + 1)
                for k in range(DVE_STEPS, STEPS):
                    at = slice(2 * k, 2 * k + 2)
                    pool.tensor_tensor(acc[:, at, :], acc[:, at, :],
                                       ln_mean.unsqueeze(1).to_broadcast([P, 2, T]), ALU.subtract)\
                        .then_inc(ln_zero_p, 1)

            residual(0, R_RO)
            norm(0)
            residual(1, R_LN0)
            norm(1)
            residual(2, R_LN1)
            norm(2)
            residual(3, R_LN2)
            norm(3)

        @block.tensor
        def _(pe):
            def turn(src, half, b, ready, between={}, last=False):
                dst = banks(half)

                def tile(c, n):
                    s = c // KCH % SPLITS
                    w = slice(c % KCH * COLS + n * P, c % KCH * COLS + (n + 1) * P)
                    pe.matmul(dst[:, n, :], wh[:, s, w], src[:, c, :, :], start=(c == 0), stop=False)
                    return pe.matmul(dst[:, n, 0:T], wl[:, s, w], src[:, c, 0, :],
                                     start=False, stop=(c == NC - 1))

                whole = BLOCKS - 2 if last else BLOCKS
                for kb in range(whole):
                    if kb in between:
                        between[kb]()
                    pe.wait_ge(pair_ready, ready + (kb + 1))
                    pe.wait_ge(wl_done, b + kb + 1)
                    for c in range(kb * KCH, (kb + 1) * KCH):
                        for n in range(GROUP):
                            mm = tile(c, n)
                    mm.then_inc(mm_done, 1)
                if last:
                    between[whole]()
                    pe.wait_ge(pair_ready, ready + BLOCKS)
                    pe.wait_ge(wl_done, b + BLOCKS)
                    for k, (first, end) in enumerate(PIECES):
                        for n in range(first, end):
                            for c in range(whole * KCH, NC):
                                mm = tile(c, n)
                        if k < 2:
                            mm.then_inc(piece_mm, 1)
                    mm.then_inc(mm_done, 2)

            def pair(src, b, ready, free):
                for j in range(2):
                    pe.wait_ge(psum_free, free + (j - 1))
                    turn(src, j, b + j * BLOCKS, ready)

            def input_pair(k):
                pe.wait_ge(x_loaded[k], 16)
                if k >= 4:
                    pe.wait_ge(pair_ready, R_X + k - 3)
                for q in range(KCH):
                    for h in range(HALVES):
                        c = k * KCH + q
                        mm = pe.transpose(xt_bank(k)[:, q, h * P:(h + 1) * P],
                                          f1[:, h * D + c * P:h * D + (c + 1) * P], ident[:, :])
                mm.then_inc(xt_done, 1)

            def parameters():
                pe.wait_ge(prm_loaded, 16 * 8)
                pe.wait_ge(pair_ready, R_X + 5)
                for k in range(2):
                    mm = pe.transpose(ps[:, 4, k * P:(k + 1) * P], f2[:, k * P:(k + 1) * P], ident[:, :])
                mm.then_inc(prm_t, 1)

            pe.wait_ge(consts, 4)
            for k in range(AHEAD_X):
                input_pair(k)
            between = {k - AHEAD_X + 1: lambda k=k: input_pair(k) for k in range(AHEAD_X, BLOCKS)}
            turn(xin, 0, B_U, R_X, {**between, BLOCKS - 1: parameters})
            pe.wait_ge(prm_ready, 1)
            turn(xin, 1, B_U + BLOCKS, R_X)
            pair(xin, B_U + 2 * BLOCKS, R_X, T_U + 2)

            for gt in range(4):
                dst = banks(gt % 2)
                if gt < 2:
                    pe.wait_ge(psum_free, T_G + gt - 1)
                else:
                    pe.wait_ge(sig_done, gt - 1)
                for half in range(2):
                    gb = 2 * gt + half
                    pe.wait_ge(pair_ready, R_CONV + 4 * (gt // 2) + 2 * half + 2)
                    pe.wait_ge(wl_done, B_GATES + gb + 1)
                    s = gb % SPLITS
                    for nl in range(2):
                        n = (gt // 2) * 4 + half * 2 + nl
                        for vc in range(2):
                            o = half * 4 + nl * 2 + vc
                            o_ap = dst[:, o // 2, (o % 2) * T:(o % 2 + 1) * T]
                            for kk in range(2):
                                w = slice((nl * 2 + kk) * LRU_W + vc * P, (nl * 2 + kk) * LRU_W + (vc + 1) * P)
                                c = 2 * n + kk
                                pe.matmul(o_ap, wh[:, s, w], hid[:, c, 0, :], start=(kk == 0), stop=False)
                                pe.matmul(o_ap, wh[:, s, w], hid[:, c, 1, :], start=False, stop=False)
                                mm = pe.matmul(o_ap, wl[:, s, w], hid[:, c, 0, :], start=False,
                                               stop=(kk == 1))
                    mm.then_inc(mm_done, 1)

            pe.wait_ge(sig_done, 3)
            with pe.Fori(0, NG // 2) as h:
                for j in range(2):
                    if j == 1:
                        pe.wait_ge(sig_done, 4)
                    pe.wait_ge(psum_free, h * 2 + (T_G + j - 1))
                    turn(xin, j, B_G + h * (2 * BLOCKS) + j * BLOCKS, R_X)

            def last_pair(src, b, ready, free, n):
                def shift():
                    pe.wait_ge(psum_free, free)
                    pe.wait_ge(ln_part, n + 1)
                    pe.matmul(ps[:, 4, 0:T], ones[:, :], ln_sum, start=True, stop=True).then_inc(ln_mm, 1)

                def mean_of(k, what, first=False, end=False):
                    return pe.matmul(ps[:, k, 0:T], ones[:, :], what, start=first, stop=end)

                def totals():
                    pe.wait_ge(psum_free, free + 1)
                    for k, total in enumerate((ln_sum, ln_sumsq)):
                        pe.wait_ge(ln_sums, 2 * n + k + 1)
                        mean_of(k, total, first=True)

                pe.wait_ge(psum_free, free - 1)
                turn(src, 0, b, ready, {BLOCKS // 2: shift})
                pe.wait_ge(psum_free, free)
                pe.wait_ge(ln_shifted, n + 1)
                turn(src, 1, b + BLOCKS, ready, {BLOCKS - 2: totals}, last=True)
                for k, what in enumerate((ln_pair, ln_pairsq)):
                    pe.wait_ge(ln_pairs, 2 * n + k + 1)
                    mean_of(k, what)
                pe.wait_ge(piece_added, 2 * n + 2)
                mean_of(0, acc[:, 14, :])
                pe.wait_ge(ln_squared, 6 * n + 5)
                mean_of(1, squares[:, 14, :])
                pe.wait_ge(psum_free, free + 2)
                mean_of(0, acc[:, 15, :], end=True).then_inc(ln_mm, 1)
                pe.wait_ge(ln_squared, 6 * n + 6)
                mean_of(1, squares[:, 15, :], end=True).then_inc(ln_mm, 1)

            def out_unit(b, ready, free, n):
                pair(hid, b, ready, free)
                last_pair(hid, b + 2 * BLOCKS, ready, free + 2, n)

            def mlp(b0, ready_x, ready_h, free, n):
                def w1(s, slabs_blocks, slabs_turns):
                    with pe.Fori(0, NG // 2) as h:
                        pair(xin, b0 + slabs_blocks + h * (2 * BLOCKS), ready_x, free + slabs_turns + h * 2)

                with pe.Fori(0, SLABS - 1) as s:
                    w1(s, s * SLAB_BLOCKS, s * (2 * NG))
                    with pe.Fori(0, NG // 2) as h:
                        pair(hid, b0 + NG * BLOCKS + s * SLAB_BLOCKS + h * (2 * BLOCKS),
                             ready_h + s * (2 * NG), free + NG + s * (2 * NG) + h * 2)
                s = SLABS - 1
                w1(s, s * SLAB_BLOCKS, s * 2 * NG)
                out = b0 + NG * BLOCKS + s * SLAB_BLOCKS
                free_out = free + NG + s * 2 * NG
                pair(hid, out, ready_h + s * (2 * NG), free_out)
                last_pair(hid, out + 2 * BLOCKS, ready_h + s * (2 * NG), free_out + 2, n)

            out_unit(B_RO, R_RO, T_RO, 0)
            mlp(B_MLP0, R_LN0, R_SQ0, T_MLP0, 1)

            with pe.Fori(0, NG // 2) as it:
                for j in range(2):
                    g = it * 2 + j
                    X, Y = banks(j), banks(1 - j)
                    b = B_QKV + it * (6 * BLOCKS) + j * (3 * BLOCKS)
                    turn(xin, j, b, R_LN1)
                    pe.wait_ge(pair_ready, it * 4 + (2 * j + R_ATT))
                    turn(xin, 1 - j, b + BLOCKS, R_LN1)
                    pe.wait_ge(qk_ready, it * 4 + 2 * j + 1)
                    for kb in range(BLOCKS):
                        if kb == BLOCKS // 2:
                            pe.wait_ge(qk_ready, it * 4 + 2 * j + 2)
                            for h in range(GROUP):
                                pe.matmul(Y[:, h, 0:P], qg[:, h, 0:P], kg[:, h, 0:P], start=True, stop=True)
                                mm = pe.matmul(Y[:, h, P:3 * P], qg[:, h, P:T], kg[:, h, :],
                                               start=True, stop=True)
                            mm.then_inc(scores_done, 1)
                        pe.wait_ge(wl_done, b + 2 * BLOCKS + kb + 1)
                        s = kb % SPLITS
                        for kk in range(KCH):
                            c = kb * KCH + kk
                            w = slice(kk * COLS, (kk + 1) * COLS)
                            for a in range(HALVES):
                                tok = slice(a * P, (a + 1) * P)
                                pe.matmul(X[:, a, :], xin[:, c, 0, tok], wh[:, s, w], start=(c == 0), stop=False)
                                pe.matmul(X[:, a, :], xin[:, c, 1, tok], wh[:, s, w], start=False, stop=False)
                                mm = pe.matmul(X[:, a, :], xin[:, c, 0, tok], wl[:, s, w], start=False,
                                               stop=(c == NC - 1))
                        mm.then_inc(mm_done, 1)
                    pe.wait_ge(p_ready, g + 1)
                    for h in range(GROUP):
                        for k in range(3):
                            mm = pe.transpose(Y[:, h, k * P:(k + 1) * P], prob[:, h, k * P:(k + 1) * P],
                                              ident[:, :])
                        mm.then_inc(pt_done, 1)
                    pe.wait_ge(v_stored, g + 1)
                    for h in range(GROUP):
                        pe.wait_ge(pt_copied, it * (2 * GROUP) + j * GROUP + h + 1)
                        o_ap = X[:, 2 + h // 2, (h % 2) * T:(h % 2 + 1) * T]
                        pe.matmul(o_ap, vg[:, 0, h * P:(h + 1) * P], probt[:, h, 0:2 * P],
                                  start=True, stop=False)
                        mm = pe.matmul(o_ap[:, P:T], vg[:, 1, h * P:(h + 1) * P], probt[:, h, 2 * P:3 * P],
                                       start=False, stop=True)
                    mm.then_inc(pv_done, 1)

            out_unit(B_MO, R_ATT, T_MO, 2)
            mlp(B_MLP1, R_LN2, R_SQ1, T_MLP1, 3)
            for k in range(STEPS):
                g = k // 2
                pe.wait_ge(ln_hi, 3 * NC + 2 * k + 2)
                if k == 0:
                    pe.wait_ge(ln_sqmean, 4)
                if k % 2 == 0 and g >= 2:
                    pe.wait_ge(out_copied, g - 1)
                for a in range(HALVES):
                    for q in range(2):
                        to = (k % 2) * 2 + q
                        mm = pe.transpose(banks(0)[:, 2 * (g % 2) + a, to * P:(to + 1) * P],
                                          acc[:, 2 * k + q, a * P:(a + 1) * P], ident[:, :])
                mm.then_inc(out_t, 1)

        @block.scalar
        def _(act):
            def split_hi(b, turn_no, off):
                kb = off % BLOCKS
                act.wait_ge(stage_full[kb], turn_no * 16 + 16 * (off // BLOCKS + 1))
                if not (isinstance(b, int) and b + off < SPLITS):
                    act.wait_ge(mm_done, b + (off - (SPLITS - 1)))
                act.activation(wh[:, off % SPLITS, :], wst[:, kb, :], ACT.Copy).then_inc(wh_done, 1)

            def splits(b, turn_no, lo=AHEAD, hi=AHEAD + BLOCKS):
                for off in range(lo, hi):
                    split_hi(b, turn_no, off)

            def take_hl(half, b, dst, done):
                act.wait_ge(mm_done, b + BLOCKS)
                act.activation(dst, banks(half)[:, :, T:2 * T], ACT.Copy).then_inc(done, 1)

            act.wait_ge(consts, 3)
            act.activation(eps[:, :], ones[:, 0:1], ACT.Copy, scale=LN_EPS * D).then_inc(eps_ready, 1)
            for k in range(BLOCKS):
                act.wait_ge(xt_done, k + 1)
                act.activation(xin[:, k * KCH:(k + 1) * KCH, 0, :], xt_bank(k), ACT.Copy).then_inc(xt_hi, 1)
                split_hi(0, 0, k)

            def conv_hi_part(g):
                act.wait_ge(conv_link, (g + 1) * (CONV - 1))
                act.activation(hid[:, g * GROUP:(g + 1) * GROUP, 0, :], e1[:, :, :], ACT.Copy)\
                   .then_inc(conv_hi, 1)

            def conv_start(g):
                act.wait_ge(psum_free, T_U + g + 1)
                if g >= 1:
                    act.wait_ge(pair_ready, R_CONV + 2 * g)
                for c in range(g * GROUP, (g + 1) * GROUP):
                    tap = C_CONVW + (CONV - 1) * NC + c
                    ins = act.activation(e1[:, c % GROUP, :], u3[:, c, :], ACT.Identity,
                                         scale=prm[:, tap:tap + 1], bias=prm[:, C_CONVB + c:C_CONVB + c + 1])
                ins.then_inc(conv_begun, 1)

            for t in range(NG):
                b = B_U + t * BLOCKS
                if t:
                    splits(b, t, AHEAD, AHEAD + 1)
                    conv_start(t - 1)
                    splits(b, t, AHEAD + 1, AHEAD + CONV)
                    if t == 1:
                        act.wait_ge(sp_abs, 1)
                        act.activation(small[:, 1, :], small[:, 0, :], ACT.Exp, scale=-1.0).then_inc(sp_exp, 1)
                    conv_hi_part(t - 1)
                splits(b, t, AHEAD + CONV, LATE)
                take_hl(t % 2, b, u3[:, t * GROUP:(t + 1) * GROUP, :], hl_copied)
                splits(b, t, LATE)
            conv_start(NG - 1)
            for gt in range(4):
                splits(B_GATES, B_GATES // BLOCKS, AHEAD + 2 * gt, AHEAD + 2 * gt + 2)
                act.wait_ge(mm_done, B_GATES + 2 * gt + 2)
                dst, bias = ((r3, C_BA), (i3, C_BX))[gt % 2]
                for o in range(8):
                    c = (gt // 2) * 8 + o
                    sg = act.activation(dst[:, c, :], banks(gt % 2)[:, o // 2, (o % 2) * T:(o % 2 + 1) * T],
                                        ACT.Sigmoid, bias=prm[:, bias + c:bias + c + 1])
                sg.then_inc(sig_done, 1)
                if gt == 0:
                    conv_hi_part(NG - 1)
            act.wait_ge(sp_ready, 1)
            act.wait_ge(sig_done, 4)

            def decay(g):
                for c in range(g * GROUP, (g + 1) * GROUP):
                    act.activation(u3[:, c, :], r3[:, c, :], ACT.Exp, scale=small[:, 6, c:c + 1])
                for c in range(g * GROUP, (g + 1) * GROUP):
                    th = act.activation(r3[:, c, :], r3[:, c, :], ACT.Tanh, scale=small[:, 7, c:c + 1])
                th.then_inc(tanh_done, 1)

            def root(g):
                act.wait_ge(tanh_done, g + 1)
                act.activation(r3[:, g * GROUP:(g + 1) * GROUP, :], r3[:, g * GROUP:(g + 1) * GROUP, :],
                               ACT.Sqrt).then_inc(rec_root, 1)

            def gelu(g):
                act.wait_ge(psum_free, T_G + g + 1)
                act.activation(acc[:, g * GROUP:(g + 1) * GROUP, :], acc[:, g * GROUP:(g + 1) * GROUP, :],
                               ACT.Gelu_apprx_tanh).then_inc(gelu_done, 1)

            def product_hi(g):
                act.wait_ge(prod_done, g + 1)
                act.activation(hid[:, g * GROUP:(g + 1) * GROUP, 0, :], acc[:, g * GROUP:(g + 1) * GROUP, :],
                               ACT.Copy).then_inc(prod_hi, 1)

            work = (((2, decay, 0), (2, decay, 1)), ((2, decay, 2), (2, decay, 3)),
                    ((1, root, 0), (0, root, 1), (1, root, 2), (1, root, 3), (2, gelu, 0), (0, gelu, 1)),
                    ((0, product_hi, 0), (2, product_hi, 1), (2, gelu, 2), (0, product_hi, 2)))
            for t in range(NG):
                b, no = B_G + t * BLOCKS, B_G // BLOCKS + t
                off = AHEAD
                for n, what, g in work[t]:
                    splits(b, no, off, off + n)
                    off += n
                    what(g)
                splits(b, no, off, LATE)
                take_hl(t % 2, b, acc[:, t * GROUP:(t + 1) * GROUP, :], hl_copied)
                splits(b, no, LATE)
            gelu(NG - 1)
            product_hi(NG - 1)
            splits(b, no, LATE + 1, NEXT)

            def last_pair(b, no, free, n, end=False):
                def square(g):
                    act.activation(squares[:, g * GROUP:(g + 1) * GROUP, :],
                                   acc[:, g * GROUP:(g + 1) * GROUP, :], ACT.Square).then_inc(ln_squared, 1)

                splits(b, no, START, BLOCKS)
                for g in range(2):
                    act.wait_ge(ln_centred, 2 * n + g + 1)
                    square(g)
                splits(b, no, BLOCKS, NEXT)
                b, no = b + BLOCKS, no + 1
                act.wait_ge(psum_free, free + 1)
                square(2)
                splits(b, no, START, BLOCKS if end else BLOCKS + 2)
                for k, (first, last) in enumerate(PIECES):
                    if k < 2:
                        act.wait_ge(piece_added, 2 * n + k + 1)
                    else:
                        act.wait_ge(psum_free, free + 2)
                    at = slice((NG - 1) * GROUP + first, (NG - 1) * GROUP + last)
                    act.activation(squares[:, at, :], acc[:, at, :], ACT.Square).then_inc(ln_squared, 1)
                act.wait_ge(ln_mm, 3 * n + 2)
                act.activation(ln_mean, ps[:, 0, 0:T], ACT.Copy).then_inc(ln_copied, 1)
                act.activation(ln_sqm, ps[:, 0, 0:T], ACT.Square).then_inc(ln_sqmean, 1)
                act.wait_ge(ln_var, n + 1)
                act.activation(ln_std, ln_var_t, ACT.Sqrt, bias=eps[:, 0:1]).then_inc(ln_root, 1)
                if not end:
                    splits(b, no, BLOCKS + 2, LATE)
                for c in range(NC):
                    act.wait_ge(ln_scaled, n * NC + c + 1)
                    act.activation(acc[:, c, :] if end else xin[:, c, 0, :], acc[:, c, :], ACT.Identity,
                                   bias=prm[:, C_LNB + n * NC + c:C_LNB + n * NC + c + 1]).then_inc(ln_hi, 1)
                    if end and c % GROUP == 1 and c > GROUP:
                        copy_out(c // GROUP - 1)
                    if not end and c in (3, 11, 15):
                        off = LATE + (3, 11, 15).index(c)
                        splits(b, no, off, off + 1)
                if end:
                    copy_out(NG - 1)

            def copy_out(g):
                act.wait_ge(out_t, 2 * g + 2)
                act.activation(f2[:, :].rearrange("p (a n) -> p a n", a=HALVES)[:, :, g * COLS:(g + 1) * COLS],
                               banks(0)[:, 2 * (g % 2):2 * (g % 2) + 2, :], ACT.Copy).then_inc(out_copied, 1)

            def out_unit(b0, free, n):
                for j in range(2):
                    splits(b0 + j * BLOCKS, b0 // BLOCKS + j, START, NEXT)
                last_pair(b0 + 2 * BLOCKS, b0 // BLOCKS + 2, free + 2, n)

            def mlp(b0, sq, free, n, end=False):
                def w1_turns(s, h):
                    for j in range(2):
                        b = b0 + s * SLAB_BLOCKS + h * (2 * BLOCKS) + j * BLOCKS
                        m = sq + s * NG + h * 2 + j
                        no = b0 // BLOCKS + s * (2 * NG) + h * 2 + j
                        splits(b, no, START, LATE)
                        take_hl(j, b, e1[:, :, :], sq_hl)
                        splits(b, no, LATE, LATE + 1)
                        act.wait_ge(sq_val, m + 1)
                        rows = bass.ds(h * (2 * GROUP) + j * GROUP, GROUP)
                        act.activation(hid[:, rows, 0, :], e2[:, :, :], ACT.Copy).then_inc(sq_hi, 1)
                        splits(b, no, LATE + 1, NEXT)

                def w2_turns(s, h):
                    for j in range(2):
                        b = b0 + NG * BLOCKS + s * SLAB_BLOCKS + h * (2 * BLOCKS) + j * BLOCKS
                        splits(b, b0 // BLOCKS + NG + s * (2 * NG) + h * 2 + j, START, NEXT)

                with act.Fori(0, SLABS - 1) as s:
                    with act.Fori(0, NG // 2) as h:
                        w1_turns(s, h)
                    with act.Fori(0, NG // 2) as h:
                        w2_turns(s, h)
                s = SLABS - 1
                with act.Fori(0, NG // 2) as h:
                    w1_turns(s, h)
                w2_turns(s, 0)
                out = b0 + NG * BLOCKS + s * SLAB_BLOCKS + 2 * BLOCKS
                last_pair(out, out // BLOCKS, free + s * 2 * NG + NG + 2, n, end)

            out_unit(B_RO, T_RO, 0)
            mlp(B_MLP0, 0, T_MLP0, 1)
            with act.Fori(0, NG // 2) as it:
                for j in range(2):
                    g = it * 2 + j
                    b = B_QKV + it * (6 * BLOCKS) + j * (3 * BLOCKS)
                    no = B_QKV // BLOCKS + it * 6 + j * 3
                    for part, dst in enumerate((qg, kg)):
                        splits(b + part * BLOCKS, no + part, START, LATE)
                        take_hl((j, 1 - j)[part], b + part * BLOCKS, dst, hl_copied)
                        splits(b + part * BLOCKS, no + part, LATE, NEXT)
                    bv, nv = b + 2 * BLOCKS, no + 2
                    splits(bv, nv, START, AHEAD + 4)
                    act.wait_ge(bias_ready, g + 1)
                    for h in range(GROUP):
                        for a, cols in enumerate((slice(0, P), slice(P, 3 * P))):
                            ex = act.activation(prob[:, h, cols], prob[:, h, cols], ACT.Exp, scale=QK_SCALE,
                                                bias=stat[:, h, 2 + a:3 + a], accum_out=stat[:, h, 4 + a:5 + a])
                    ex.then_inc(exp_done, 1)
                    splits(bv, nv, AHEAD + 4, LATE)
                    act.wait_ge(mm_done, bv + BLOCKS)
                    act.activation(vg, banks(j)[:, 0:2, :], ACT.Copy).then_inc(v_stored, 1)
                    for h in range(GROUP):
                        act.wait_ge(pt_done, it * (2 * GROUP) + j * GROUP + h + 1)
                        act.activation(probt[:, h, :], banks(1 - j)[:, h, 0:3 * P], ACT.Copy)\
                           .then_inc(pt_copied, 1)
                    act.wait_ge(pv_done, g + 1)
                    act.activation(hid[:, bass.ds(g * GROUP, GROUP), 0, :],
                                   banks(j)[:, 2:4, :].rearrange("p b (c t) -> p (b c) t", t=T),
                                   ACT.Copy).then_inc(pv_hi, 1)
                    splits(bv, nv, LATE, NEXT)
            out_unit(B_MO, T_MO, 2)
            mlp(B_MLP1, SLABS * NG, T_MLP1, 3, end=True)

        @block.vector
        def _(dve):
            def split_lo(b, off):
                dve.wait_ge(wh_done, b + (off + 1))
                if not (isinstance(b, int) and b + off < SPLITS):
                    dve.wait_ge(mm_done, b + (off - (SPLITS - 1)))
                dve.tensor_tensor(wl[:, off % SPLITS, :], wst[:, off % BLOCKS, :], wh[:, off % SPLITS, :],
                                  ALU.subtract).then_inc(wl_done, 1)

            def splits(b, lo=AHEAD, hi=AHEAD + BLOCKS):
                for off in range(lo, hi):
                    split_lo(b, off)

            def add_hh(half, dst, copied, n):
                dve.wait_ge(copied, n)
                return dve.tensor_tensor(dst, dst, banks(half)[:, :, 0:T], ALU.add)

            for k in range(BLOCKS):
                rows = slice(k * KCH, (k + 1) * KCH)
                dve.wait_ge(xt_hi, k + 1)
                dve.tensor_tensor(xin[:, rows, 1, :], xt_bank(k), xin[:, rows, 0, :], ALU.subtract)\
                   .then_inc(pair_ready, 1)
                split_lo(0, k)

            links = [0]

            def link(ins):
                links[0] += 1
                ins.then_inc(sp_link, 1)
                dve.wait_ge(sp_link, links[0])

            lam = prm[:, C_LAM:C_LAM + NC]
            absl, y, den, s, z, p, neg8, pos4 = (small[:, k, :] for k in range(8))

            def softplus_abs():
                dve.wait_ge(prm_t, 1)
                dve.tensor_copy(prm[:, :], ps[:, 4, 0:256]).then_inc(prm_ready, 1)
                dve.wait_ge(prm_ready, 1)
                link(dve.tensor_scalar(den, lam, -1.0, None, ALU.mult))
                dve.tensor_tensor(absl, lam, den, ALU.max).then_inc(sp_abs, 1)

            def softplus_start():
                dve.wait_ge(sp_exp, 1)
                link(dve.tensor_scalar(den, y, 2.0, None, ALU.add))
                link(dve.reciprocal(den, den))
                link(dve.tensor_tensor(s, y, den, ALU.mult))
                link(dve.tensor_tensor(z, s, s, ALU.mult))
                link(dve.tensor_scalar(p, z, 1.0 / 17, None, ALU.mult))

            def softplus_series():
                for k in range(15, 1, -2):
                    link(dve.scalar_tensor_tensor(out=p, in0=p, scalar=1.0 / k, in1=z, op0=ALU.add,
                                                  op1=ALU.mult))
                link(dve.scalar_tensor_tensor(out=p, in0=p, scalar=1.0, in1=s, op0=ALU.add, op1=ALU.mult))
                link(dve.tensor_scalar(den, lam, -1.0, 0.0, ALU.mult, ALU.max))
                link(dve.scalar_tensor_tensor(out=p, in0=p, scalar=2.0, in1=den, op0=ALU.mult, op1=ALU.add))
                link(dve.tensor_scalar(neg8, p, -LRU_C, None, ALU.mult))
                dve.tensor_scalar(pos4, p, LRU_C / 2, None, ALU.mult).then_inc(sp_ready, 1)

            def conv_step(g, k):
                if k == 1:
                    dve.wait_ge(conv_begun, g + 1)
                else:
                    dve.wait_ge(conv_link, g * (CONV - 1) + k - 1)
                for q in range(GROUP):
                    c = g * GROUP + q
                    col = C_CONVW + (CONV - 1 - k) * NC + c
                    ins = dve.scalar_tensor_tensor(out=e1[:, q, k:T], in0=u3[:, c, 0:T - k],
                                                   scalar=prm[:, col:col + 1], in1=e1[:, q, k:T],
                                                   op0=ALU.mult, op1=ALU.add)
                ins.then_inc(conv_link, 1)

            def conv_lo(g):
                rows = slice(g * GROUP, (g + 1) * GROUP)
                dve.wait_ge(conv_hi, g + 1)
                dve.tensor_tensor(hid[:, rows, 1, :], e1[:, :, :], hid[:, rows, 0, :], ALU.subtract)\
                   .then_inc(pair_ready, 2)

            for t in range(NG):
                b = B_U + t * BLOCKS
                if t:
                    splits(b, AHEAD, AHEAD + 1)
                    for k in range(1, CONV):
                        splits(b, AHEAD + k, AHEAD + k + 1)
                        conv_step(t - 1, k)
                    splits(b, AHEAD + CONV, AHEAD + CONV + 1)
                    conv_lo(t - 1)
                    splits(b, AHEAD + CONV + 1, LATE)
                else:
                    splits(b, BLOCKS, LATE)
                (softplus_abs, softplus_start, softplus_series, lambda: None)[t]()
                add_hh(t % 2, u3[:, t * GROUP:(t + 1) * GROUP, :], hl_copied, t + 1).then_inc(psum_free, 1)
                splits(b, LATE)
            g = NG - 1
            for k in range(1, CONV):
                conv_step(g, k)
            splits(B_GATES, AHEAD, AHEAD + 1)
            conv_lo(g)
            splits(B_GATES, AHEAD + 1)

            def root(g):
                rows = slice(g * GROUP, (g + 1) * GROUP)
                dve.wait_ge(rec_root, g + 1)
                dve.scalar_tensor_tensor(out=r3[:, rows, :], in0=u3[:, rows, :], scalar=1.0,
                                         in1=r3[:, rows, :], op0=ALU.add, op1=ALU.mult).then_inc(rec_link, 1)

            def states(g):
                dve.wait_ge(b_ready, g + 1)
                for c in range(g * GROUP, (g + 1) * GROUP):
                    ins = dve.tensor_tensor_scan(out=r3[:, c, :], data0=u3[:, c, :], data1=i3[:, c, :],
                                                 initial=0.0, op0=ALU.mult, op1=ALU.add)
                ins.then_inc(h_ready, 1)

            def product(g):
                rows = slice(g * GROUP, (g + 1) * GROUP)
                dve.wait_ge(h_ready, g + 1)
                dve.wait_ge(gelu_done, g + 1)
                dve.tensor_tensor(acc[:, rows, :], acc[:, rows, :], r3[:, rows, :], ALU.mult)\
                   .then_inc(prod_done, 1)

            def product_lo(g):
                rows = slice(g * GROUP, (g + 1) * GROUP)
                dve.wait_ge(prod_hi, g + 1)
                dve.tensor_tensor(hid[:, rows, 1, :], acc[:, rows, :], hid[:, rows, 0, :], ALU.subtract)\
                   .then_inc(pair_ready, 2)

            work = ((), (),
                    ((1, root, 0), (0, root, 1), (1, root, 2), (0, root, 3), (1, states, 0), (1, states, 1)),
                    ((0, product, 0), (0, product_lo, 0), (1, states, 2), (0, product, 1), (1, product_lo, 1),
                     (1, states, 3), (0, product, 2), (1, product_lo, 2)))
            for t in range(NG):
                b = B_G + t * BLOCKS
                off = AHEAD
                for n, what, g in work[t]:
                    splits(b, off, off + n)
                    off += n
                    what(g)
                splits(b, off, LATE)
                add_hh(t % 2, acc[:, t * GROUP:(t + 1) * GROUP, :], hl_copied, T_G + t + 1)\
                    .then_inc(psum_free, 1)
                splits(b, LATE)
            product(NG - 1)
            product_lo(NG - 1)
            splits(b, LATE + 1, NEXT)

            def add_turn(half, b, rows, n):
                dve.wait_ge(mm_done, b + BLOCKS)
                dve.tensor_tensor(acc[:, rows, :], acc[:, rows, :], banks(half)[:, :, 0:T], ALU.add)\
                   .then_inc(acc_half, 1)
                dve.wait_ge(acc_half, n + 1)
                dve.tensor_tensor(acc[:, rows, :], acc[:, rows, :], banks(half)[:, :, T:2 * T], ALU.add)\
                   .then_inc(psum_free, 1)

            def last_pair(b, use, n0, free, n, end=False):
                rows = [slice(g * GROUP, (g + 1) * GROUP) for g in range(NG)]
                dve.wait_ge(psum_free, free)
                dve.wait_ge(acc_ready, NG * use + NG)
                dve.tensor_reduce(ln_sum, acc[:, 0:2 * GROUP, :].rearrange("p c t -> p t c"), AX_X, ALU.add)\
                   .then_inc(ln_part, 1)
                splits(b, START, START + 2)
                dve.wait_ge(ln_mm, 3 * n + 1)
                dve.tensor_scalar(ln_shift, ps[:, 4, 0:T], float(NC) / (2 * GROUP), None, ALU.mult)\
                   .then_inc(ln_shifted, 1)
                dve.wait_ge(ln_shifted, n + 1)
                for g in range(NG):
                    if g == 2:
                        splits(b, START + 2, START + 3)
                    dve.tensor_tensor(acc[:, rows[g], :], acc[:, rows[g], :],
                                      ln_shift.unsqueeze(1).to_broadcast([P, GROUP, T]), ALU.subtract)\
                       .then_inc(ln_centred if g < 2 else ln_late, 1)
                splits(b, START + 3, LATE)
                dve.wait_ge(ln_late, 2 * n + 2)
                add_turn(0, b, rows[2], n0)
                splits(b, LATE, NEXT)
                b += BLOCKS
                dve.wait_ge(psum_free, free + 1)
                dve.tensor_reduce(ln_sum, acc[:, 0:3 * GROUP, :].rearrange("p c t -> p t c"), AX_X, ALU.add)\
                   .then_inc(ln_sums, 1)
                splits(b, START, START + 1)
                dve.wait_ge(ln_squared, 6 * n + 3)
                dve.tensor_reduce(ln_sumsq, squares[:, 0:3 * GROUP, :].rearrange("p c t -> p t c"),
                                  AX_X, ALU.add).then_inc(ln_sums, 1)
                splits(b, START + 1, BLOCKS if end else BLOCKS + 2)
                for k, (first, last) in enumerate(PIECES):
                    if k < 2:
                        dve.wait_ge(piece_mm, 2 * n + k + 1)
                    else:
                        dve.wait_ge(mm_done, b + BLOCKS)
                    piece = slice(rows[3].start + first, rows[3].start + last)
                    dve.tensor_tensor(acc[:, piece, :], acc[:, piece, :], banks(1)[:, first:last, 0:T], ALU.add)\
                       .then_inc(piece_half, 1)
                    dve.wait_ge(piece_half, 3 * n + k + 1)
                    dve.tensor_tensor(acc[:, piece, :], acc[:, piece, :],
                                      banks(1)[:, first:last, T:2 * T], ALU.add)\
                       .then_inc(piece_added if k < 2 else psum_free, 1)

                def centre(k):
                    at = slice(2 * k, 2 * k + 2)
                    dve.tensor_tensor(acc[:, at, :], acc[:, at, :],
                                      ln_mean.unsqueeze(1).to_broadcast([P, 2, T]), ALU.subtract)\
                       .then_inc(ln_zero, 1)

                def scale(k):
                    if k < DVE_STEPS:
                        dve.wait_ge(ln_zero, DVE_STEPS * n + k + 1)
                    else:
                        dve.wait_ge(ln_zero_p, (STEPS - DVE_STEPS) * n + k - DVE_STEPS + 1)
                    for c in (2 * k, 2 * k + 1):
                        col = C_LNG + n * NC + c
                        dve.scalar_tensor_tensor(out=acc[:, c, :], in0=acc[:, c, :], scalar=prm[:, col:col + 1],
                                                 in1=ln_rstd, op0=ALU.mult, op1=ALU.mult).then_inc(ln_scaled, 1)

                def lo(k):
                    for c in (2 * k, 2 * k + 1):
                        dve.wait_ge(ln_hi, n * NC + c + 1)
                        col = C_LNB + n * NC + c
                        ins = dve.scalar_tensor_tensor(out=xin[:, c, 1, :], in0=acc[:, c, :],
                                                       scalar=prm[:, col:col + 1], in1=xin[:, c, 0, :],
                                                       op0=ALU.add, op1=ALU.subtract)
                    ins.then_inc(pair_ready, 1)

                dve.wait_ge(psum_free, free + 2)
                dve.wait_ge(ln_sqmean, n + 1)
                dve.wait_ge(ln_mm, 3 * n + 3)
                dve.tensor_tensor(ln_var_t, ps[:, 1, 0:T], ln_sqm, ALU.subtract).then_inc(ln_var, 1)
                dve.wait_ge(ln_copied, n + 1)
                centre(0)
                dve.wait_ge(ln_root, n + 1)
                dve.reciprocal(ln_rstd, ln_std).then_inc(ln_inv, 1)
                dve.wait_ge(ln_inv, n + 1)
                for k in range(STEPS):
                    scale(k)
                    if not end and k != 1:
                        lo(k - 1 if k else 0)
                    if k < DVE_STEPS - 1:
                        centre(k + 1)
                    if not end and k in (1, 2):
                        splits(b, BLOCKS + 1 + k, BLOCKS + 2 + k)
                    if not end and k == STEPS - 1:
                        splits(b, LATE + 1, LATE + 2)
                if not end:
                    lo(STEPS - 1)
                    splits(b, LATE + 2, NEXT)

            def out_unit(b0, use, n0, free, n):
                for t in range(2):
                    b = b0 + t * BLOCKS
                    splits(b, START, LATE)
                    dve.wait_ge(acc_ready, NG * use + t + 1)
                    add_turn(t, b, slice(t * GROUP, (t + 1) * GROUP), n0 + t)
                    splits(b, LATE, NEXT)
                last_pair(b0 + 2 * BLOCKS, use, n0 + 2, free + 2, n)

            def mlp(b0, sq, use, n0, free, n, end=False):
                def w1_turns(s, h):
                    for j in range(2):
                        b = b0 + s * SLAB_BLOCKS + h * (2 * BLOCKS) + j * BLOCKS
                        m = sq + s * NG + h * 2 + j
                        rows = bass.ds(h * (2 * GROUP) + j * GROUP, GROUP)
                        splits(b, START, LATE)
                        add_hh(j, e1[:, :, :], sq_hl, m + 1).then_inc(psum_free, 1)
                        dve.wait_ge(psum_free, free + s * (2 * NG) + h * 2 + (j + 1))
                        dve.scalar_tensor_tensor(out=e2[:, :, :], in0=e1[:, :, :], scalar=0.0, in1=e1[:, :, :],
                                                 op0=ALU.max, op1=ALU.mult).then_inc(sq_val, 1)
                        splits(b, LATE, LATE + 1)
                        dve.wait_ge(sq_hi, m + 1)
                        dve.tensor_tensor(hid[:, rows, 1, :], e2[:, :, :], hid[:, rows, 0, :], ALU.subtract)\
                           .then_inc(pair_ready, 2)
                        splits(b, LATE + 1, NEXT)

                def w2_turns(s, h):
                    for j in range(2):
                        b = b0 + NG * BLOCKS + s * SLAB_BLOCKS + h * (2 * BLOCKS) + j * BLOCKS
                        splits(b, START, LATE)
                        dve.wait_ge(acc_ready, NG * use + NG)
                        add_turn(j, b, bass.ds(h * (2 * GROUP) + j * GROUP, GROUP),
                                 n0 + s * NG + h * 2 + j)
                        splits(b, LATE, NEXT)

                with dve.Fori(0, SLABS - 1) as s:
                    with dve.Fori(0, NG // 2) as h:
                        w1_turns(s, h)
                    with dve.Fori(0, NG // 2) as h:
                        w2_turns(s, h)
                s = SLABS - 1
                with dve.Fori(0, NG // 2) as h:
                    w1_turns(s, h)
                w2_turns(s, 0)
                last_pair(b0 + NG * BLOCKS + s * SLAB_BLOCKS + 2 * BLOCKS, use, n0 + s * NG + 2,
                          free + s * 2 * NG + NG + 2, n, end)

            out_unit(B_RO, 0, 0, T_RO, 0)
            mlp(B_MLP0, 0, 1, NG - 1, T_MLP0, 1)

            cos_t = ropet[:, 0:1, :].to_broadcast([32, GROUP, T])
            sin_t = ropet[:, 1:2, :].to_broadcast([32, GROUP, T])
            swap = [k ^ ROPE_HALF for k in range(32)]
            dve.wait_ge(consts, 6)
            with dve.Fori(0, NG // 2) as it:
                for j in range(2):
                    g = it * 2 + j
                    b = B_QKV + it * (6 * BLOCKS) + j * (3 * BLOCKS)
                    for part, dst in enumerate((qg, kg)):
                        splits(b + part * BLOCKS, START, LATE)
                        links = it * 12 + 6 * j + 3 * part
                        n = it * 4 + 2 * j + part
                        add_hh((j, 1 - j)[part], dst, hl_copied, T_RO + n + 1).then_inc(qk_link, 1)
                        dve.wait_ge(qk_link, links + 1)
                        dve.tensor_tensor(cosd[0:32, :, :], dst[0:32, :, :], cos_t, ALU.mult)
                        dve.stream_shuffle(rot[0:32, :, :], dst[0:32, :, :], swap).then_inc(qk_link, 1)
                        dve.wait_ge(qk_link, links + 2)
                        dve.tensor_tensor(rot[0:32, :, :], rot[0:32, :, :], sin_t, ALU.mult)\
                           .then_inc(qk_link, 1)
                        dve.wait_ge(qk_link, links + 3)
                        splits(b + part * BLOCKS, LATE, LATE + 1)
                        dve.tensor_tensor(dst[0:32, :, :], cosd[0:32, :, :], rot[0:32, :, :], ALU.add)\
                           .then_inc(qk_ready, 1)
                        splits(b + part * BLOCKS, LATE + 1, NEXT)
                    bv = b + 2 * BLOCKS
                    al = it * 6 + 3 * j
                    splits(bv, START, AHEAD + 3)
                    dve.wait_ge(scores_done, g + 1)
                    dve.tensor_tensor(prob, banks(1 - j)[:, :, 0:3 * P],
                                      maskt[:, :].unsqueeze(1).to_broadcast([P, GROUP, 3 * P]), ALU.add)\
                       .then_inc(att_link, 1)
                    dve.wait_ge(att_link, al + 1)
                    dve.tensor_reduce(stat[:, :, 0:1], prob[:, :, 0:P], AX_X, ALU.max)
                    dve.tensor_reduce(stat[:, :, 1:2], prob[:, :, P:3 * P], AX_X, ALU.max)\
                       .then_inc(att_link, 1)
                    dve.wait_ge(att_link, al + 2)
                    dve.tensor_scalar(stat[:, :, 2:4], stat[:, :, 0:2], -QK_SCALE, None, ALU.mult)\
                       .then_inc(bias_ready, 1)
                    splits(bv, AHEAD + 3, AHEAD + 4)
                    dve.wait_ge(exp_done, g + 1)
                    dve.reciprocal(stat[:, :, 6:8], stat[:, :, 4:6]).then_inc(att_link, 1)
                    dve.wait_ge(att_link, al + 3)
                    dve.tensor_tensor(prob[:, :, 0:P], prob[:, :, 0:P],
                                      stat[:, :, 6:7].to_broadcast([P, GROUP, P]), ALU.mult)
                    dve.tensor_tensor(prob[:, :, P:3 * P], prob[:, :, P:3 * P],
                                      stat[:, :, 7:8].to_broadcast([P, GROUP, 2 * P]), ALU.mult)\
                       .then_inc(p_ready, 1)
                    splits(bv, AHEAD + 4, LATE)
                    dve.wait_ge(pv_hi, g + 1)
                    rows = bass.ds(g * GROUP, GROUP)
                    dve.tensor_tensor(hid[:, rows, 1, :],
                                      banks(j)[:, 2:4, :].rearrange("p b (c t) -> p (b c) t", t=T),
                                      hid[:, rows, 0, :], ALU.subtract).then_inc(pair_ready, 2)
                    splits(bv, LATE, NEXT)
            out_unit(B_MO, 2, (NG - 1) + (SLABS * NG - 1), T_MO, 2)
            mlp(B_MLP1, SLABS * NG, 3, 2 * (NG - 1) + (SLABS * NG - 1), T_MLP1, 3, end=True)


_INS = ["x", "ln_g", "ln_b", "mlp_w1", "mlp_w2", "rg_w_in", "rg_conv_w", "rg_conv_b", "rg_gate_a_w",
        "rg_gate_a_b", "rg_gate_x_w", "rg_gate_x_b", "rg_lambda", "rg_w_out", "moba_w_qkv", "moba_w_out"]


def rope_table():
    inv = np.float32(500000.0) ** (-np.arange(0, 32, 2, dtype=np.float32) / np.float32(32))
    ang = np.arange(T, dtype=np.float32)[None, :] * inv.astype(np.float32)[:, None]
    cos, sin = np.cos(ang).astype(np.float32), np.sin(ang).astype(np.float32)
    return np.stack([np.concatenate([cos, cos]), np.concatenate([-sin, sin])], axis=1)


def kernel(**inputs):
    import concourse.bacc as _bacc
    from concourse.bass_utils import run_bass_kernel_spmd as _run

    nc = _bacc.Bacc("TRN2", target_bir_lowering=False, num_devices=1)
    arrays, args = {}, []
    given = {n: inputs[n] for n in _INS}
    given["rope"] = rope_table()
    for name, value in given.items():
        a = np.ascontiguousarray(value)
        arrays[f"in_{name}_dram"] = a
        args.append(nc.dram_tensor(f"in_{name}_dram", a.shape, mybir.dt.from_np(a.dtype),
                                   kind="ExternalInput").ap())
    out = nc.dram_tensor("out_dram", (1, T, D), F32, kind="ExternalOutput").ap()
    build_trunk(nc, *args, out)
    r = _run(nc, [arrays], core_ids=[0])
    return r.results[0]["out_dram"]
```

```python
from contextlib import ExitStack

import numpy as np

import concourse.bass as bass
from concourse import mybir

F32 = mybir.dt.float32
F32R = mybir.dt.float32r
ALU = mybir.AluOpType
ACT = mybir.ActivationFunctionType
AX_X = mybir.AxisListType.X

P = 128
T = 256
D = 2048
NC = D // P
HALVES = T // P
GROUP = 4
NG = NC // GROUP
COLS = GROUP * P
KCH = 2
BLOCKS = NC // KCH
BLK = KCH * COLS
SPLITS = 4
AHEAD = 4
D_FF = 8192
SLABS = D_FF // D
LRU_BLOCKS = 8
LRU_W = D // LRU_BLOCKS
CONV = 4
LRU_C = 8.0
ROPE_HALF = 16
DEPTH = 2
ALPHA = (2.0 * DEPTH) ** 0.25
LN_EPS = 1e-5
QK_SCALE = 128 ** -0.5
NEG = -1e30

B_U = 0
B_GATES = B_U + NG * BLOCKS
B_G = B_GATES + BLOCKS
B_RO = B_G + NG * BLOCKS
B_MLP0 = B_RO + NG * BLOCKS
B_QKV = B_MLP0 + 2 * SLABS * NG * BLOCKS
B_MO = B_QKV + 3 * NG * BLOCKS
B_MLP1 = B_MO + NG * BLOCKS
SLAB_BLOCKS = 2 * NG * BLOCKS

T_U, T_G, T_RO, T_MLP0, T_MO, T_MLP1 = 0, 4, 8, 12, 44, 48

R_X, R_CONV, R_RO, R_LN0, R_SQ0, R_LN1, R_ATT, R_LN2, R_SQ1 = 0, 8, 16, 24, 32, 64, 72, 80, 88
AHEAD_X = 2
LATE = AHEAD + BLOCKS - 1
START = AHEAD + 2
NEXT = LATE + 3
STEPS = NC // 2
UNITS = tuple((g, h, ("pool", "pool", "both")[g] if h == 1 and g < 3 else "dve")
              for g in range(NG) for h in range(HALVES))
PIECES = ((0, 2), (2, 3), (3, 4))

C_LNG, C_LNB, C_CONVW, C_CONVB, C_BA, C_BX, C_LAM = 0, 64, 128, 192, 208, 224, 240


def build_trunk(nc, x, ln_g, ln_b, mlp_w1, mlp_w2, rg_w_in, rg_conv_w, rg_conv_b, rg_gate_a_w,
                rg_gate_a_b, rg_gate_x_w, rg_gate_x_b, rg_lambda, rg_w_out, moba_w_qkv, moba_w_out,
                rope, out):
    with ExitStack() as ctx:
        def sb(name, shape, dt=F32):
            return ctx.enter_context(nc.sbuf_tensor(name, shape, dt))

        def sem(name):
            return ctx.enter_context(nc.semaphore(name))

        xin = sb("xin", [P, NC, 2, T], F32R)
        hid = sb("hid", [P, NC, 2, T], F32R)
        acc = sb("acc", [P, NC, T])
        f1 = sb("f1", [P, NC * T])
        f2 = sb("f2", [P, NC * T])
        f3 = sb("f3", [P, NC * T])
        e1 = sb("e1", [P, GROUP, T])
        e2 = sb("e2", [P, GROUP, T])
        wst = sb("wst", [P, BLOCKS, BLK])
        wh = sb("wh", [P, SPLITS, BLK], F32R)
        wl = sb("wl", [P, SPLITS, BLK], F32R)
        prm = sb("prm", [P, 256])
        ident = sb("ident", [P, P])
        eps = sb("eps", [P, 1])
        ones = sb("ones", [P, P])
        maskt = sb("maskt", [P, 3 * P])
        ropet = sb("ropet", [32, 2, T])
        small = sb("small", [P, 8, NC])
        tok = sb("tok", [P, 6, HALVES, 1])
        stat = sb("stat", [P, 4, 8])
        ps = ctx.enter_context(nc.psum_tensor("ps", [P, 8, 512], F32))

        u3 = f1[:, :].rearrange("p (c t) -> p c t", t=T)
        r3 = f2[:, :].rearrange("p (c t) -> p c t", t=T)
        i3 = f3[:, :].rearrange("p (c t) -> p c t", t=T)
        qg = f1[:, 0:1024].rearrange("p (c t) -> p c t", t=T)
        kg = f1[:, 1024:2048].rearrange("p (c t) -> p c t", t=T)
        vg = f1[:, 2048:3072].rearrange("p (a n) -> p a n", a=HALVES)
        rot = f1[:, 3072:4096].rearrange("p (c t) -> p c t", t=T)
        cosd = f2[:, 3072:4096].rearrange("p (c t) -> p c t", t=T)
        prob = f2[:, 0:1536].rearrange("p (h n) -> p h n", n=3 * P)
        probt = f2[:, 1536:3072].rearrange("p (h n) -> p h n", n=3 * P)
        (ln_shift, ln_sum, ln_sum4, ln_sumsq, ln_pair, ln_pairsq, ln_mean, ln_sqm, ln_var_t, ln_std, ln_rstd) = \
            (f3[:, k * T:(k + 1) * T] for k in range(11))
        gain_row, bias_row = f2[:, 0:D], f2[:, D:2 * D]
        out_tok = f1[:, :].rearrange("p (a n) -> p a n", a=HALVES)
        squares = f1[:, :].rearrange("p (c t) -> p c t", t=T)

        stage_full = [sem(f"stage_full{s}") for s in range(BLOCKS)]
        x_loaded = [sem(f"x_loaded{k}") for k in range(BLOCKS)]
        prm_loaded = sem("prm_loaded")
        wh_done = sem("wh_done")
        wl_done = sem("wl_done")
        mm_done = sem("mm_done")
        pair_ready = sem("pair_ready")
        psum_free = sem("psum_free")
        xt_done = sem("xt_done")
        xt_hi = sem("xt_hi")
        eps_ready = sem("eps_ready")
        consts = sem("consts")
        prm_t = sem("prm_t")
        prm_ready = sem("prm_ready")
        sp_link = sem("sp_link")
        sp_abs = sem("sp_abs")
        sp_exp = sem("sp_exp")
        sp_ready = sem("sp_ready")
        hl_copied = sem("hl_copied")
        conv_begun = sem("conv_begun")
        conv_link = sem("conv_link")
        conv_hi = sem("conv_hi")
        sig_done = sem("sig_done")
        ui_sum = sem("ui_sum")
        b_ready = sem("b_ready")
        ui_ready = sem("ui_ready")
        tanh_done = sem("tanh_done")
        rec_root = sem("rec_root")
        rec_link = sem("rec_link")
        h_ready = sem("h_ready")
        gelu_done = sem("gelu_done")
        prod_done = sem("prod_done")
        prod_hi = sem("prod_hi")
        acc_half = sem("acc_half")
        pool_sum = sem("pool_sum")
        acc_ready = sem("acc_ready")
        sq_hl = sem("sq_hl")
        sq_val = sem("sq_val")
        sq_hi = sem("sq_hi")
        ln_part = sem("ln_part")
        ln_mm = sem("ln_mm")
        ln_shifted = sem("ln_shifted")
        ln_centred = sem("ln_centred")
        ln_late = sem("ln_late")
        ln_squared = sem("ln_squared")
        ln_link = sem("ln_link")
        sq_added = sem("sq_added")
        ln_sums = sem("ln_sums")
        piece_mm = sem("piece_mm")
        piece_half = sem("piece_half")
        piece_added = sem("piece_added")
        ln_pairs = sem("ln_pairs")
        ln_sqmean = sem("ln_sqmean")
        ln_copied = sem("ln_copied")
        ln_var = sem("ln_var")
        ln_root = sem("ln_root")
        ln_inv = sem("ln_inv")
        ln_zero = sem("ln_zero")
        ln_zero_p = sem("ln_zero_p")
        ln_scaled = sem("ln_scaled")
        ln_hi = sem("ln_hi")
        qk_link = sem("qk_link")
        qk_ready = sem("qk_ready")
        scores_done = sem("scores_done")
        att_link = sem("att_link")
        bias_ready = sem("bias_ready")
        exp_done = sem("exp_done")
        p_ready = sem("p_ready")
        v_stored = sem("v_stored")
        pt_done = sem("pt_done")
        pt_copied = sem("pt_copied")
        pv_done = sem("pv_done")
        pv_hi = sem("pv_hi")
        rows_loaded = sem("rows_loaded")
        tok_bias = sem("tok_bias")
        out_t = sem("out_t")
        out_norm = sem("out_norm")
        out_link = sem("out_link")
        out_link_p = sem("out_link_p")
        out_dve = sem("out_dve")
        out_pool = sem("out_pool")
        stored = sem("stored")

        def banks(half):
            return ps[:, 4 * half:4 * half + 4, :]

        def out_bank(g, h):
            return ps[:, (4, 6, 0, 2)[g] + h, :]

        def xt_bank(k):
            return ps[:, 4 + k % 4, :].rearrange("p (c t) -> p c t", t=T)

        def cols_of(w, first):
            return w.rearrange("(b k p) n -> b p k n", k=KCH, p=P)[:, :, :, bass.ds(first, COLS)]

        block = ctx.enter_context(nc.Block())

        @block.sync
        def _(sp):
            def load_block(src, kb, b):
                if b is not None:
                    sp.wait_ge(wl_done, b - (BLOCKS - 1))
                sp.dma_start(wst[:, kb, :].rearrange("p (k n) -> p k n", k=KCH), src)\
                  .then_inc(stage_full[kb], 16)

            def load_turn(w, col, b):
                col = sp.snap(col)
                src = cols_of(w, col)
                for kb in range(BLOCKS):
                    load_block(src[kb], kb, b + kb)

            w_in = rg_w_in[0]
            first = cols_of(w_in, D)
            x_tok = f1[:, :].rearrange("p (a n) -> p a n", a=HALVES)
            x_src = x[0].rearrange("(a p) n -> p a n", p=P)
            for kb in range(BLOCKS):
                pair = slice(kb * KCH * P, (kb + 1) * KCH * P)
                sp.dma_start(x_tok[:, :, pair], x_src[:, :, pair]).then_inc(x_loaded[kb], 16)
                load_block(first[kb], kb, None)
            for dst, src in ((f2[0:64, 0:P], ln_g.rearrange("a b (c p) -> (a b c) p", p=P)),
                             (f2[64:128, 0:P], ln_b.rearrange("a b (c p) -> (a b c) p", p=P)),
                             (f2[0:64, P:2 * P], rg_conv_w.rearrange("l k (c p) -> (l k c) p", p=P)),
                             (f2[64:80, P:2 * P], rg_conv_b.rearrange("l (c p) -> (l c) p", p=P)),
                             (f2[80:96, P:2 * P], rg_gate_a_b.rearrange("l n (c p) -> (l n c) p", p=P)),
                             (f2[96:112, P:2 * P], rg_gate_x_b.rearrange("l n (c p) -> (l n c) p", p=P)),
                             (f2[112:128, P:2 * P], rg_lambda.rearrange("l (c p) -> (l c) p", p=P)),
                             (ropet[:, :, :], rope)):
                sp.dma_start(dst, src).then_inc(prm_loaded, 16)
            with sp.Fori(1, NG) as t:
                load_turn(w_in, D + t * COLS, B_U + t * BLOCKS)
            for gb in range(BLOCKS):
                w = (rg_gate_a_w, rg_gate_x_w)[(gb // 2) % 2]
                n0 = (gb // 4) * 4 + (gb % 2) * 2
                sp.wait_ge(wl_done, B_GATES + gb - (BLOCKS - 1))
                sp.dma_start(wst[:, gb, :].rearrange("p (k n) -> p k n", n=LRU_W),
                             w[0, n0:n0 + 2].rearrange("n (k p) v -> p (n k) v", p=P))\
                  .then_inc(stage_full[gb], 16)
            with sp.Fori(0, NG) as t:
                load_turn(w_in, t * COLS, B_G + t * BLOCKS)
            with sp.Fori(0, NG) as t:
                load_turn(rg_w_out[0], t * COLS, B_RO + t * BLOCKS)

            def load_mlp(layer, b0):
                with sp.Fori(0, SLABS) as s:
                    with sp.Fori(0, NG) as t:
                        load_turn(mlp_w1[layer], s * D + t * COLS,
                                  b0 + s * SLAB_BLOCKS + t * BLOCKS)
                    w2 = mlp_w2[layer].rearrange("(s r) n -> s r n", r=D)
                    with sp.Fori(0, NG) as t:
                        b = b0 + NG * BLOCKS + s * SLAB_BLOCKS + t * BLOCKS
                        slab = sp.snap(s + 0)
                        col = sp.snap(t * COLS)
                        for kb in range(BLOCKS):
                            src = w2[bass.ds(slab, 1), kb * KCH * P:(kb + 1) * KCH * P,
                                     bass.ds(col, COLS)]
                            load_block(src.rearrange("s (k p) n -> p (s k) n", p=P), kb, b + kb)

            load_mlp(0, B_MLP0)
            with sp.Fori(0, NG) as g:
                for part in range(3):
                    load_turn(moba_w_qkv[0], part * D + g * COLS,
                              B_QKV + (3 * g + part) * BLOCKS)
            with sp.Fori(0, NG) as t:
                load_turn(moba_w_out[0], t * COLS, B_MO + t * BLOCKS)
            load_mlp(1, B_MLP1)
            last = ln_g.shape[1] - 1
            for dst, src in ((gain_row, ln_g), (bias_row, ln_b)):
                sp.dma_start(dst, src[DEPTH - 1, last:last + 1, :].to_broadcast([P, D])).then_inc(rows_loaded, 16)
            count = {"dve": 0, "pool": 0}
            for g, h, who in sorted(UNITS, key=lambda unit: unit[2] == "both"):
                who = who.replace("both", "dve")
                count[who] += 1
                if who == "dve":
                    sp.wait_ge(out_dve, count[who])
                else:
                    sp.wait_ge(out_pool, count[who])
                cols = slice(g * COLS, (g + 1) * COLS)
                sp.dma_start(out[0, h * P:(h + 1) * P, cols], out_tok[:, h, cols]).then_inc(stored, 16)
            sp.wait_ge(stored, 16 * len(UNITS))

        @block.gpsimd
        def _(pool):
            pool.memset(ident[:, :], 0.0).then_inc(consts, 1)
            pool.memset(ones[:, :], 1.0 / D).then_inc(consts, 1)
            pool.memset(maskt[:, :], 0.0).then_inc(consts, 1)
            pool.wait_ge(consts, 3)
            pool.affine_select(out=ident[:, :], in_=ident[:, :], compare_op=ALU.not_equal, fill=1.0,
                               base=0, pattern=[[-1, P]], channel_multiplier=1).then_inc(consts, 1)
            for lo, base, n in ((0, 0, P), (P, P, 2 * P)):
                pool.affine_select(out=maskt[:, lo:lo + n], in_=maskt[:, lo:lo + n],
                                   compare_op=ALU.is_ge, fill=NEG, base=base,
                                   pattern=[[-1, n]], channel_multiplier=1).then_inc(consts, 1)

            pool.wait_ge(sig_done, 4)
            for g in range(NG):
                rows = slice(g * GROUP, (g + 1) * GROUP)
                if g >= 1:
                    pool.wait_ge(ui_ready, g)
                pool.tensor_tensor(e1[:, :, :], hid[:, rows, 0, :], hid[:, rows, 1, :], ALU.add)\
                    .then_inc(ui_sum, 1)
                pool.wait_ge(ui_sum, g + 1)
                pool.tensor_tensor(i3[:, rows, :], i3[:, rows, :], e1[:, :, :], ALU.mult)\
                    .then_inc(ui_ready, 1)

            for g in range(NG):
                rows = slice(g * GROUP, (g + 1) * GROUP)
                pool.wait_ge(rec_link, g + 1)
                pool.wait_ge(ui_ready, g + 1)
                pool.tensor_tensor(i3[:, rows, :], i3[:, rows, :], r3[:, rows, :], ALU.mult)\
                    .then_inc(b_ready, 1)

            def residual(use, ready):
                for g in range(NG):
                    rows = slice(g * GROUP, (g + 1) * GROUP)
                    pool.wait_ge(pair_ready, ready + 2 * g + 2)
                    pool.tensor_tensor(acc[:, rows, :], xin[:, rows, 0, :], xin[:, rows, 1, :],
                                       ALU.add).then_inc(pool_sum, 1)
                    pool.wait_ge(pool_sum, use * NG + g + 1)
                    pool.tensor_scalar(acc[:, rows, :], acc[:, rows, :], ALPHA, None, ALU.mult)\
                        .then_inc(acc_ready, 1)

            def norm(n):
                for k in range(1, NG - 1):
                    pool.wait_ge(ln_squared, 6 * n + k + 1)
                    if k == 2:
                        pool.wait_ge(sq_added, 2 * n + 1)
                    pool.tensor_tensor(squares[:, 0:GROUP, :], squares[:, 0:GROUP, :],
                                       squares[:, k * GROUP:(k + 1) * GROUP, :], ALU.add).then_inc(sq_added, 1)
                pool.wait_ge(piece_added, 2 * n + 1)
                c = (NG - 1) * GROUP
                pool.tensor_tensor(ln_pair, acc[:, c, :], acc[:, c + 1, :], ALU.add).then_inc(ln_pairs, 1)
                pool.wait_ge(ln_squared, 6 * n + 4)
                pool.tensor_tensor(ln_pairsq, squares[:, c, :], squares[:, c + 1, :], ALU.add)\
                    .then_inc(ln_pairs, 1)
                if n == 3:
                    return
                pool.wait_ge(ln_copied, n + 1)
                for k in range(1, STEPS):
                    at = slice(2 * k, 2 * k + 2)
                    pool.tensor_tensor(acc[:, at, :], acc[:, at, :],
                                       ln_mean.unsqueeze(1).to_broadcast([P, 2, T]), ALU.subtract)\
                        .then_inc(ln_zero_p, 1)

            residual(0, R_RO)
            norm(0)
            residual(1, R_LN0)
            norm(1)
            residual(2, R_LN1)
            norm(2)
            residual(3, R_LN2)
            norm(3)
            pool.wait_ge(rows_loaded, 32)
            for k, (g, h, who) in enumerate([unit for unit in UNITS if unit[2] != "dve"]):
                cols = slice(g * COLS, (g + 1) * COLS)
                pool.wait_ge(out_norm, k + 1)
                pool.tensor_tensor(out_tok[:, h, cols], out_tok[:, h, cols], gain_row[:, cols], ALU.mult)\
                    .then_inc(out_link_p, 1)
                if who == "both":
                    continue
                pool.wait_ge(out_link_p, k + 1)
                pool.tensor_tensor(out_tok[:, h, cols], out_tok[:, h, cols], bias_row[:, cols], ALU.add)\
                    .then_inc(out_pool, 1)

        @block.tensor
        def _(pe):
            def turn(src, half, b, ready, between={}, last=False):
                dst = banks(half)

                def tile(c, n):
                    s = c // KCH % SPLITS
                    w = slice(c % KCH * COLS + n * P, c % KCH * COLS + (n + 1) * P)
                    pe.matmul(dst[:, n, :], wh[:, s, w], src[:, c, :, :], start=(c == 0), stop=False)
                    return pe.matmul(dst[:, n, 0:T], wl[:, s, w], src[:, c, 0, :],
                                     start=False, stop=(c == NC - 1))

                whole = BLOCKS - 2 if last else BLOCKS
                for kb in range(whole):
                    if kb in between:
                        between[kb]()
                    pe.wait_ge(pair_ready, ready + (kb + 1))
                    pe.wait_ge(wl_done, b + kb + 1)
                    for c in range(kb * KCH, (kb + 1) * KCH):
                        for n in range(GROUP):
                            mm = tile(c, n)
                    mm.then_inc(mm_done, 1)
                if last:
                    between[whole]()
                    pe.wait_ge(pair_ready, ready + BLOCKS)
                    pe.wait_ge(wl_done, b + BLOCKS)
                    for k, (first, end) in enumerate(PIECES):
                        for n in range(first, end):
                            for c in range(whole * KCH, NC):
                                mm = tile(c, n)
                        if k < 2:
                            mm.then_inc(piece_mm, 1)
                    mm.then_inc(mm_done, 2)

            def pair(src, b, ready, free):
                for j in range(2):
                    pe.wait_ge(psum_free, free + (j - 1))
                    turn(src, j, b + j * BLOCKS, ready)

            def input_pair(k):
                pe.wait_ge(x_loaded[k], 16)
                if k >= 4:
                    pe.wait_ge(pair_ready, R_X + k - 3)
                for q in range(KCH):
                    for h in range(HALVES):
                        c = k * KCH + q
                        mm = pe.transpose(xt_bank(k)[:, q, h * P:(h + 1) * P],
                                          f1[:, h * D + c * P:h * D + (c + 1) * P], ident[:, :])
                mm.then_inc(xt_done, 1)

            def parameters():
                pe.wait_ge(prm_loaded, 16 * 8)
                pe.wait_ge(pair_ready, R_X + 5)
                for k in range(2):
                    mm = pe.transpose(ps[:, 4, k * P:(k + 1) * P], f2[:, k * P:(k + 1) * P], ident[:, :])
                mm.then_inc(prm_t, 1)

            def keep_warm(times):
                for _ in range(times):
                    pe.matmul(ps[:, 7, 0:P], ones[:, :], ones[:, :], start=True, stop=True)

            pe.wait_ge(consts, 4)
            keep_warm(3)
            for k in range(AHEAD_X):
                input_pair(k)
                keep_warm(3 - k)
            between = {k - AHEAD_X + 1: lambda k=k: input_pair(k) for k in range(AHEAD_X, BLOCKS)}
            turn(xin, 0, B_U, R_X, {**between, BLOCKS - 1: parameters})
            pe.wait_ge(prm_ready, 1)
            turn(xin, 1, B_U + BLOCKS, R_X)
            pair(xin, B_U + 2 * BLOCKS, R_X, T_U + 2)

            for gt in range(4):
                dst = banks(gt % 2)
                if gt < 2:
                    pe.wait_ge(psum_free, T_G + gt - 1)
                else:
                    pe.wait_ge(sig_done, gt - 1)
                for half in range(2):
                    gb = 2 * gt + half
                    pe.wait_ge(pair_ready, R_CONV + 4 * (gt // 2) + 2 * half + 2)
                    pe.wait_ge(wl_done, B_GATES + gb + 1)
                    s = gb % SPLITS
                    for nl in range(2):
                        n = (gt // 2) * 4 + half * 2 + nl
                        for vc in range(2):
                            o = half * 4 + nl * 2 + vc
                            o_ap = dst[:, o // 2, (o % 2) * T:(o % 2 + 1) * T]
                            for kk in range(2):
                                w = slice((nl * 2 + kk) * LRU_W + vc * P, (nl * 2 + kk) * LRU_W + (vc + 1) * P)
                                c = 2 * n + kk
                                pe.matmul(o_ap, wh[:, s, w], hid[:, c, 0, :], start=(kk == 0), stop=False)
                                pe.matmul(o_ap, wh[:, s, w], hid[:, c, 1, :], start=False, stop=False)
                                mm = pe.matmul(o_ap, wl[:, s, w], hid[:, c, 0, :], start=False,
                                               stop=(kk == 1))
                    mm.then_inc(mm_done, 1)

            pe.wait_ge(sig_done, 3)
            with pe.Fori(0, NG // 2) as h:
                for j in range(2):
                    if j == 1:
                        pe.wait_ge(sig_done, 4)
                    pe.wait_ge(psum_free, h * 2 + (T_G + j - 1))
                    turn(xin, j, B_G + h * (2 * BLOCKS) + j * BLOCKS, R_X)

            def last_pair(src, b, ready, free, n):
                def shift():
                    pe.wait_ge(psum_free, free)
                    pe.wait_ge(ln_part, n + 1)
                    pe.matmul(ps[:, 4, 0:T], ones[:, :], ln_sum, start=True, stop=True).then_inc(ln_mm, 1)

                def mean_of(k, what, first=False, end=False):
                    if n < 3:
                        return pe.matmul(ps[:, k, 0:T], ones[:, :], what, start=first, stop=end)
                    for h in range(HALVES):
                        mm = pe.matmul(ps[:, 2 * k + h, 0:1], what[:, h * P:(h + 1) * P], ones[:, 0:1],
                                       start=first, stop=end)
                    return mm

                def totals():
                    pe.wait_ge(psum_free, free + 1)
                    for k, total in enumerate((ln_sum, ln_sumsq)):
                        pe.wait_ge(ln_sums, 2 * n + k + 1)
                        mean_of(k, total, first=True)

                pe.wait_ge(psum_free, free - 1)
                turn(src, 0, b, ready, {BLOCKS // 2: shift})
                pe.wait_ge(psum_free, free)
                pe.wait_ge(ln_shifted, n + 1)
                turn(src, 1, b + BLOCKS, ready, {BLOCKS - 2: totals}, last=True)
                pe.wait_ge(ln_pairs, 2 * n + 1)
                mean_of(0, ln_pair)
                pe.wait_ge(piece_added, 2 * n + 2)
                mean_of(0, acc[:, NC - 2, :])
                pe.wait_ge(ln_pairs, 2 * n + 2)
                mean_of(1, ln_pairsq)
                pe.wait_ge(ln_squared, 6 * n + 5)
                mean_of(1, squares[:, NC - 2, :])
                pe.wait_ge(psum_free, free + 2)
                mean_of(0, acc[:, NC - 1, :], end=True).then_inc(ln_mm, 1)
                pe.wait_ge(ln_squared, 6 * n + 6)
                mean_of(1, squares[:, NC - 1, :], end=True).then_inc(ln_mm, 1)
                if n < 3:
                    keep_warm(4)
                    for done, count, times in ((ln_var, n + 1, 2), (ln_root, n + 1, 6), (ln_inv, n + 1, 2),
                                               (ln_scaled, n * NC + 2, 2), (ln_hi, n * NC + 1, 2)):
                        pe.wait_ge(done, count)
                        keep_warm(times)

            def out_unit(b, ready, free, n):
                pair(hid, b, ready, free)
                last_pair(hid, b + 2 * BLOCKS, ready, free + 2, n)

            def mlp(b0, ready_x, ready_h, free, n):
                def w1(s, slabs_blocks, slabs_turns):
                    with pe.Fori(0, NG // 2) as h:
                        pair(xin, b0 + slabs_blocks + h * (2 * BLOCKS), ready_x, free + slabs_turns + h * 2)

                with pe.Fori(0, SLABS - 1) as s:
                    w1(s, s * SLAB_BLOCKS, s * (2 * NG))
                    with pe.Fori(0, NG // 2) as h:
                        pair(hid, b0 + NG * BLOCKS + s * SLAB_BLOCKS + h * (2 * BLOCKS),
                             ready_h + s * (2 * NG), free + NG + s * (2 * NG) + h * 2)
                s = SLABS - 1
                w1(s, s * SLAB_BLOCKS, s * 2 * NG)
                out = b0 + NG * BLOCKS + s * SLAB_BLOCKS
                free_out = free + NG + s * 2 * NG
                pair(hid, out, ready_h + s * (2 * NG), free_out)
                last_pair(hid, out + 2 * BLOCKS, ready_h + s * (2 * NG), free_out + 2, n)

            out_unit(B_RO, R_RO, T_RO, 0)
            mlp(B_MLP0, R_LN0, R_SQ0, T_MLP0, 1)

            with pe.Fori(0, NG // 2) as it:
                for j in range(2):
                    g = it * 2 + j
                    X, Y = banks(j), banks(1 - j)
                    b = B_QKV + it * (6 * BLOCKS) + j * (3 * BLOCKS)
                    turn(xin, j, b, R_LN1)
                    pe.wait_ge(pair_ready, it * 4 + (2 * j + R_ATT))
                    turn(xin, 1 - j, b + BLOCKS, R_LN1)
                    pe.wait_ge(qk_ready, it * 4 + 2 * j + 1)
                    for kb in range(BLOCKS):
                        if kb == BLOCKS // 2:
                            pe.wait_ge(qk_ready, it * 4 + 2 * j + 2)
                            for h in range(GROUP):
                                pe.matmul(Y[:, h, 0:P], qg[:, h, 0:P], kg[:, h, 0:P], start=True, stop=True)
                                mm = pe.matmul(Y[:, h, P:3 * P], qg[:, h, P:T], kg[:, h, :],
                                               start=True, stop=True)
                            mm.then_inc(scores_done, 1)
                        pe.wait_ge(wl_done, b + 2 * BLOCKS + kb + 1)
                        s = kb % SPLITS
                        for kk in range(KCH):
                            c = kb * KCH + kk
                            w = slice(kk * COLS, (kk + 1) * COLS)
                            for a in range(HALVES):
                                tok = slice(a * P, (a + 1) * P)
                                pe.matmul(X[:, a, :], xin[:, c, 0, tok], wh[:, s, w], start=(c == 0), stop=False)
                                pe.matmul(X[:, a, :], xin[:, c, 1, tok], wh[:, s, w], start=False, stop=False)
                                mm = pe.matmul(X[:, a, :], xin[:, c, 0, tok], wl[:, s, w], start=False,
                                               stop=(c == NC - 1))
                        mm.then_inc(mm_done, 1)
                    pe.wait_ge(p_ready, g + 1)
                    for h in range(GROUP):
                        for k in range(3):
                            mm = pe.transpose(Y[:, h, k * P:(k + 1) * P], prob[:, h, k * P:(k + 1) * P],
                                              ident[:, :])
                        mm.then_inc(pt_done, 1)
                    pe.wait_ge(v_stored, g + 1)
                    for h in range(GROUP):
                        pe.wait_ge(pt_copied, it * (2 * GROUP) + j * GROUP + h + 1)
                        o_ap = X[:, 2 + h // 2, (h % 2) * T:(h % 2 + 1) * T]
                        pe.matmul(o_ap, vg[:, 0, h * P:(h + 1) * P], probt[:, h, 0:2 * P],
                                  start=True, stop=False)
                        mm = pe.matmul(o_ap[:, P:T], vg[:, 1, h * P:(h + 1) * P], probt[:, h, 2 * P:3 * P],
                                       start=False, stop=True)
                    mm.then_inc(pv_done, 1)

            out_unit(B_MO, R_ATT, T_MO, 2)
            mlp(B_MLP1, R_LN2, R_SQ1, T_MLP1, 3)
            for g, h, _who in UNITS:
                if (g, h) == (2, 0):
                    pe.wait_ge(ln_sqmean, 4)
                if (g, h) == (3, 0):
                    pe.wait_ge(ln_var, 4)
                for k in range(GROUP):
                    mm = pe.transpose(out_bank(g, h)[:, k * P:(k + 1) * P],
                                      acc[:, g * GROUP + k, h * P:(h + 1) * P], ident[:, :])
                mm.then_inc(out_t, 1)

        @block.scalar
        def _(act):
            def split_hi(b, turn_no, off):
                kb = off % BLOCKS
                act.wait_ge(stage_full[kb], turn_no * 16 + 16 * (off // BLOCKS + 1))
                if not (isinstance(b, int) and b + off < SPLITS):
                    act.wait_ge(mm_done, b + (off - (SPLITS - 1)))
                act.activation(wh[:, off % SPLITS, :], wst[:, kb, :], ACT.Copy).then_inc(wh_done, 1)

            def splits(b, turn_no, lo=AHEAD, hi=AHEAD + BLOCKS):
                for off in range(lo, hi):
                    split_hi(b, turn_no, off)

            def take_hl(half, b, dst, done):
                act.wait_ge(mm_done, b + BLOCKS)
                act.activation(dst, banks(half)[:, :, T:2 * T], ACT.Copy).then_inc(done, 1)

            act.wait_ge(consts, 3)
            act.activation(eps[:, :], ones[:, 0:1], ACT.Copy, scale=LN_EPS * D).then_inc(eps_ready, 1)
            for k in range(BLOCKS):
                act.wait_ge(xt_done, k + 1)
                act.activation(xin[:, k * KCH:(k + 1) * KCH, 0, :], xt_bank(k), ACT.Copy).then_inc(xt_hi, 1)
                split_hi(0, 0, k)

            def conv_hi_part(g):
                act.wait_ge(conv_link, (g + 1) * (CONV - 1))
                act.activation(hid[:, g * GROUP:(g + 1) * GROUP, 0, :], e1[:, :, :], ACT.Copy)\
                   .then_inc(conv_hi, 1)

            def conv_start(g):
                act.wait_ge(psum_free, T_U + g + 1)
                if g >= 1:
                    act.wait_ge(pair_ready, R_CONV + 2 * g)
                for c in range(g * GROUP, (g + 1) * GROUP):
                    tap = C_CONVW + (CONV - 1) * NC + c
                    ins = act.activation(e1[:, c % GROUP, :], u3[:, c, :], ACT.Identity,
                                         scale=prm[:, tap:tap + 1], bias=prm[:, C_CONVB + c:C_CONVB + c + 1])
                ins.then_inc(conv_begun, 1)

            for t in range(NG):
                b = B_U + t * BLOCKS
                if t:
                    splits(b, t, AHEAD, AHEAD + 1)
                    conv_start(t - 1)
                    splits(b, t, AHEAD + 1, AHEAD + CONV)
                    if t == 1:
                        act.wait_ge(sp_abs, 1)
                        act.activation(small[:, 1, :], small[:, 0, :], ACT.Exp, scale=-1.0).then_inc(sp_exp, 1)
                    conv_hi_part(t - 1)
                splits(b, t, AHEAD + CONV, LATE)
                take_hl(t % 2, b, u3[:, t * GROUP:(t + 1) * GROUP, :], hl_copied)
                splits(b, t, LATE)
            conv_start(NG - 1)
            for gt in range(4):
                splits(B_GATES, B_GATES // BLOCKS, AHEAD + 2 * gt, AHEAD + 2 * gt + 1)
                act.wait_ge(mm_done, B_GATES + 2 * gt + 2)
                dst, bias = ((r3, C_BA), (i3, C_BX))[gt % 2]
                for o in range(8):
                    c = (gt // 2) * 8 + o
                    sg = act.activation(dst[:, c, :], banks(gt % 2)[:, o // 2, (o % 2) * T:(o % 2 + 1) * T],
                                        ACT.Sigmoid, bias=prm[:, bias + c:bias + c + 1])
                sg.then_inc(sig_done, 1)
                if gt == 0:
                    conv_hi_part(NG - 1)
                splits(B_GATES, B_GATES // BLOCKS, AHEAD + 2 * gt + 1, AHEAD + 2 * gt + 2)
            act.wait_ge(sp_ready, 1)
            act.wait_ge(sig_done, 4)

            def decay(g):
                for c in range(g * GROUP, (g + 1) * GROUP):
                    act.activation(u3[:, c, :], r3[:, c, :], ACT.Exp, scale=small[:, 6, c:c + 1])
                for c in range(g * GROUP, (g + 1) * GROUP):
                    th = act.activation(r3[:, c, :], r3[:, c, :], ACT.Tanh, scale=small[:, 7, c:c + 1])
                th.then_inc(tanh_done, 1)

            def root(g):
                act.wait_ge(tanh_done, g + 1)
                act.activation(r3[:, g * GROUP:(g + 1) * GROUP, :], r3[:, g * GROUP:(g + 1) * GROUP, :],
                               ACT.Sqrt).then_inc(rec_root, 1)

            def gelu(g):
                act.wait_ge(psum_free, T_G + g + 1)
                act.activation(acc[:, g * GROUP:(g + 1) * GROUP, :], acc[:, g * GROUP:(g + 1) * GROUP, :],
                               ACT.Gelu_apprx_tanh).then_inc(gelu_done, 1)

            def product_hi(g):
                act.wait_ge(prod_done, g + 1)
                act.activation(hid[:, g * GROUP:(g + 1) * GROUP, 0, :], acc[:, g * GROUP:(g + 1) * GROUP, :],
                               ACT.Copy).then_inc(prod_hi, 1)

            work = (((2, decay, 0), (2, decay, 1)), ((2, decay, 2), (2, decay, 3)),
                    ((1, root, 0), (0, root, 1), (1, root, 2), (1, root, 3), (2, gelu, 0), (0, gelu, 1)),
                    ((0, product_hi, 0), (2, product_hi, 1), (2, gelu, 2), (0, product_hi, 2)))
            for t in range(NG):
                b, no = B_G + t * BLOCKS, B_G // BLOCKS + t
                off = AHEAD
                for n, what, g in work[t]:
                    splits(b, no, off, off + n)
                    off += n
                    what(g)
                splits(b, no, off, LATE)
                take_hl(t % 2, b, acc[:, t * GROUP:(t + 1) * GROUP, :], hl_copied)
                splits(b, no, LATE)
            gelu(NG - 1)
            product_hi(NG - 1)
            splits(b, no, LATE + 1, NEXT)

            act.wait_ge(eps_ready, 1)

            def last_pair(b, no, free, n, end=False):
                def square(g):
                    act.activation(squares[:, g * GROUP:(g + 1) * GROUP, :],
                                   acc[:, g * GROUP:(g + 1) * GROUP, :], ACT.Square).then_inc(ln_squared, 1)

                splits(b, no, START, BLOCKS)
                for g in range(2):
                    act.wait_ge(ln_centred, 2 * n + g + 1)
                    square(g)
                splits(b, no, BLOCKS, NEXT)
                b, no = b + BLOCKS, no + 1
                act.wait_ge(psum_free, free + 1)
                square(2)
                splits(b, no, START, BLOCKS if end else BLOCKS + 2)
                for k, (first, last) in enumerate(PIECES):
                    if k < 2:
                        act.wait_ge(piece_added, 2 * n + k + 1)
                    else:
                        act.wait_ge(psum_free, free + 2)
                    at = slice((NG - 1) * GROUP + first, (NG - 1) * GROUP + last)
                    act.activation(squares[:, at, :], acc[:, at, :], ACT.Square).then_inc(ln_squared, 1)
                act.wait_ge(ln_mm, 3 * n + 2)
                if end:
                    mean, total, squared, var, std = ps[:, 0:2, 0:1], tok[:, 0], tok[:, 1], tok[:, 2], tok[:, 3]
                else:
                    mean, total, squared, var, std = ps[:, 0, 0:T], ln_mean, ln_sqm, ln_var_t, ln_std
                act.activation(total, mean, ACT.Copy).then_inc(ln_copied, 1)
                act.activation(squared, mean, ACT.Square).then_inc(ln_sqmean, 1)
                act.wait_ge(ln_var, n + 1)
                act.activation(std, var, ACT.Sqrt, bias=eps[:, 0:1]).then_inc(ln_root, 1)
                if end:
                    act.wait_ge(tok_bias, 1)
                    for k, (g, h, who) in enumerate(UNITS):
                        if who != "dve":
                            act.wait_ge(out_t, k + 1)
                            act.activation(out_tok[:, h, g * COLS:(g + 1) * COLS], out_bank(g, h), ACT.Identity,
                                           scale=tok[:, 4, h, :], bias=tok[:, 5, h, :]).then_inc(out_norm, 1)
                    return
                splits(b, no, BLOCKS + 2, LATE)
                for c in range(NC):
                    act.wait_ge(ln_scaled, n * NC + c + 1)
                    act.activation(xin[:, c, 0, :], acc[:, c, :], ACT.Identity,
                                   bias=prm[:, C_LNB + n * NC + c:C_LNB + n * NC + c + 1]).then_inc(ln_hi, 1)
                    if c in (3, 9, 11):
                        off = LATE + (3, 9, 11).index(c)
                        splits(b, no, off, off + 1)

            def out_unit(b0, free, n):
                for j in range(2):
                    splits(b0 + j * BLOCKS, b0 // BLOCKS + j, START, NEXT)
                last_pair(b0 + 2 * BLOCKS, b0 // BLOCKS + 2, free + 2, n)

            def mlp(b0, sq, free, n, end=False):
                def w1_turns(s, h):
                    for j in range(2):
                        b = b0 + s * SLAB_BLOCKS + h * (2 * BLOCKS) + j * BLOCKS
                        m = sq + s * NG + h * 2 + j
                        no = b0 // BLOCKS + s * (2 * NG) + h * 2 + j
                        splits(b, no, START, LATE)
                        take_hl(j, b, e1[:, :, :], sq_hl)
                        splits(b, no, LATE, LATE + 1)
                        act.wait_ge(sq_val, m + 1)
                        rows = bass.ds(h * (2 * GROUP) + j * GROUP, GROUP)
                        act.activation(hid[:, rows, 0, :], e2[:, :, :], ACT.Copy).then_inc(sq_hi, 1)
                        splits(b, no, LATE + 1, NEXT)

                def w2_turns(s, h):
                    for j in range(2):
                        b = b0 + NG * BLOCKS + s * SLAB_BLOCKS + h * (2 * BLOCKS) + j * BLOCKS
                        splits(b, b0 // BLOCKS + NG + s * (2 * NG) + h * 2 + j, START, NEXT)

                with act.Fori(0, SLABS - 1) as s:
                    with act.Fori(0, NG // 2) as h:
                        w1_turns(s, h)
                    with act.Fori(0, NG // 2) as h:
                        w2_turns(s, h)
                s = SLABS - 1
                with act.Fori(0, NG // 2) as h:
                    w1_turns(s, h)
                w2_turns(s, 0)
                out = b0 + NG * BLOCKS + s * SLAB_BLOCKS + 2 * BLOCKS
                last_pair(out, out // BLOCKS, free + s * 2 * NG + NG + 2, n, end)

            out_unit(B_RO, T_RO, 0)
            mlp(B_MLP0, 0, T_MLP0, 1)
            with act.Fori(0, NG // 2) as it:
                for j in range(2):
                    g = it * 2 + j
                    b = B_QKV + it * (6 * BLOCKS) + j * (3 * BLOCKS)
                    no = B_QKV // BLOCKS + it * 6 + j * 3
                    for part, dst in enumerate((qg, kg)):
                        splits(b + part * BLOCKS, no + part, START, LATE)
                        take_hl((j, 1 - j)[part], b + part * BLOCKS, dst, hl_copied)
                        splits(b + part * BLOCKS, no + part, LATE, NEXT)
                    bv, nv = b + 2 * BLOCKS, no + 2
                    splits(bv, nv, START, AHEAD + 4)
                    act.wait_ge(bias_ready, g + 1)
                    for h in range(GROUP):
                        for a, cols in enumerate((slice(0, P), slice(P, 3 * P))):
                            ex = act.activation(prob[:, h, cols], prob[:, h, cols], ACT.Exp, scale=QK_SCALE,
                                                bias=stat[:, h, 2 + a:3 + a], accum_out=stat[:, h, 4 + a:5 + a])
                    ex.then_inc(exp_done, 1)
                    splits(bv, nv, AHEAD + 4, LATE)
                    act.wait_ge(mm_done, bv + BLOCKS)
                    act.activation(vg, banks(j)[:, 0:2, :], ACT.Copy).then_inc(v_stored, 1)
                    for h in range(GROUP):
                        act.wait_ge(pt_done, it * (2 * GROUP) + j * GROUP + h + 1)
                        act.activation(probt[:, h, :], banks(1 - j)[:, h, 0:3 * P], ACT.Copy)\
                           .then_inc(pt_copied, 1)
                    act.wait_ge(pv_done, g + 1)
                    act.activation(hid[:, bass.ds(g * GROUP, GROUP), 0, :],
                                   banks(j)[:, 2:4, :].rearrange("p b (c t) -> p (b c) t", t=T),
                                   ACT.Copy).then_inc(pv_hi, 1)
                    splits(bv, nv, LATE, NEXT)
            out_unit(B_MO, T_MO, 2)
            mlp(B_MLP1, SLABS * NG, T_MLP1, 3, end=True)

        @block.vector
        def _(dve):
            def split_lo(b, off):
                dve.wait_ge(wh_done, b + (off + 1))
                if not (isinstance(b, int) and b + off < SPLITS):
                    dve.wait_ge(mm_done, b + (off - (SPLITS - 1)))
                dve.tensor_tensor(wl[:, off % SPLITS, :], wst[:, off % BLOCKS, :], wh[:, off % SPLITS, :],
                                  ALU.subtract).then_inc(wl_done, 1)

            def splits(b, lo=AHEAD, hi=AHEAD + BLOCKS):
                for off in range(lo, hi):
                    split_lo(b, off)

            def add_hh(half, dst, copied, n):
                dve.wait_ge(copied, n)
                return dve.tensor_tensor(dst, dst, banks(half)[:, :, 0:T], ALU.add)

            for k in range(BLOCKS):
                rows = slice(k * KCH, (k + 1) * KCH)
                dve.wait_ge(xt_hi, k + 1)
                dve.tensor_tensor(xin[:, rows, 1, :], xt_bank(k), xin[:, rows, 0, :], ALU.subtract)\
                   .then_inc(pair_ready, 1)
                split_lo(0, k)

            links = [0]

            def link(ins):
                links[0] += 1
                ins.then_inc(sp_link, 1)
                dve.wait_ge(sp_link, links[0])

            lam = prm[:, C_LAM:C_LAM + NC]
            absl, y, den, s, z, p, neg8, pos4 = (small[:, k, :] for k in range(8))

            def softplus_abs():
                dve.wait_ge(prm_t, 1)
                dve.tensor_copy(prm[:, :], ps[:, 4, 0:256]).then_inc(prm_ready, 1)
                dve.wait_ge(prm_ready, 1)
                link(dve.tensor_scalar(den, lam, -1.0, None, ALU.mult))
                dve.tensor_tensor(absl, lam, den, ALU.max).then_inc(sp_abs, 1)

            def softplus_start():
                dve.wait_ge(sp_exp, 1)
                link(dve.tensor_scalar(den, y, 2.0, None, ALU.add))
                link(dve.reciprocal(den, den))
                link(dve.tensor_tensor(s, y, den, ALU.mult))
                link(dve.tensor_tensor(z, s, s, ALU.mult))
                link(dve.tensor_scalar(p, z, 1.0 / 17, None, ALU.mult))

            def softplus_series():
                for k in range(15, 1, -2):
                    link(dve.scalar_tensor_tensor(out=p, in0=p, scalar=1.0 / k, in1=z, op0=ALU.add,
                                                  op1=ALU.mult))
                link(dve.scalar_tensor_tensor(out=p, in0=p, scalar=1.0, in1=s, op0=ALU.add, op1=ALU.mult))
                link(dve.tensor_scalar(den, lam, -1.0, 0.0, ALU.mult, ALU.max))
                link(dve.scalar_tensor_tensor(out=p, in0=p, scalar=2.0, in1=den, op0=ALU.mult, op1=ALU.add))
                link(dve.tensor_scalar(neg8, p, -LRU_C, None, ALU.mult))
                dve.tensor_scalar(pos4, p, LRU_C / 2, None, ALU.mult).then_inc(sp_ready, 1)

            def conv_step(g, k):
                if k == 1:
                    dve.wait_ge(conv_begun, g + 1)
                else:
                    dve.wait_ge(conv_link, g * (CONV - 1) + k - 1)
                for q in range(GROUP):
                    c = g * GROUP + q
                    col = C_CONVW + (CONV - 1 - k) * NC + c
                    ins = dve.scalar_tensor_tensor(out=e1[:, q, k:T], in0=u3[:, c, 0:T - k],
                                                   scalar=prm[:, col:col + 1], in1=e1[:, q, k:T],
                                                   op0=ALU.mult, op1=ALU.add)
                ins.then_inc(conv_link, 1)

            def conv_lo(g):
                rows = slice(g * GROUP, (g + 1) * GROUP)
                dve.wait_ge(conv_hi, g + 1)
                dve.tensor_tensor(hid[:, rows, 1, :], e1[:, :, :], hid[:, rows, 0, :], ALU.subtract)\
                   .then_inc(pair_ready, 2)

            for t in range(NG):
                b = B_U + t * BLOCKS
                if t:
                    splits(b, AHEAD, AHEAD + 1)
                    for k in range(1, CONV):
                        splits(b, AHEAD + k, AHEAD + k + 1)
                        conv_step(t - 1, k)
                    splits(b, AHEAD + CONV, AHEAD + CONV + 1)
                    conv_lo(t - 1)
                    splits(b, AHEAD + CONV + 1, LATE)
                else:
                    softplus_abs()
                    splits(b, BLOCKS, LATE)
                (lambda: None, softplus_start, softplus_series, lambda: None)[t]()
                add_hh(t % 2, u3[:, t * GROUP:(t + 1) * GROUP, :], hl_copied, t + 1).then_inc(psum_free, 1)
                splits(b, LATE)
            g = NG - 1
            for k in range(1, CONV):
                conv_step(g, k)
            splits(B_GATES, AHEAD, AHEAD + 1)
            conv_lo(g)
            splits(B_GATES, AHEAD + 1)

            def root(g):
                rows = slice(g * GROUP, (g + 1) * GROUP)
                dve.wait_ge(rec_root, g + 1)
                dve.scalar_tensor_tensor(out=r3[:, rows, :], in0=u3[:, rows, :], scalar=1.0,
                                         in1=r3[:, rows, :], op0=ALU.add, op1=ALU.mult).then_inc(rec_link, 1)

            def states(g):
                dve.wait_ge(b_ready, g + 1)
                for c in range(g * GROUP, (g + 1) * GROUP):
                    ins = dve.tensor_tensor_scan(out=r3[:, c, :], data0=u3[:, c, :], data1=i3[:, c, :],
                                                 initial=0.0, op0=ALU.mult, op1=ALU.add)
                ins.then_inc(h_ready, 1)

            def product(g):
                rows = slice(g * GROUP, (g + 1) * GROUP)
                dve.wait_ge(h_ready, g + 1)
                dve.wait_ge(gelu_done, g + 1)
                dve.tensor_tensor(acc[:, rows, :], acc[:, rows, :], r3[:, rows, :], ALU.mult)\
                   .then_inc(prod_done, 1)

            def product_lo(g):
                rows = slice(g * GROUP, (g + 1) * GROUP)
                dve.wait_ge(prod_hi, g + 1)
                dve.tensor_tensor(hid[:, rows, 1, :], acc[:, rows, :], hid[:, rows, 0, :], ALU.subtract)\
                   .then_inc(pair_ready, 2)

            work = ((), (),
                    ((1, root, 0), (0, root, 1), (1, root, 2), (0, root, 3), (1, states, 0), (1, states, 1)),
                    ((0, product, 0), (0, product_lo, 0), (1, states, 2), (0, product, 1), (1, product_lo, 1),
                     (1, states, 3), (0, product, 2), (1, product_lo, 2)))
            for t in range(NG):
                b = B_G + t * BLOCKS
                off = AHEAD
                for n, what, g in work[t]:
                    splits(b, off, off + n)
                    off += n
                    what(g)
                splits(b, off, LATE)
                add_hh(t % 2, acc[:, t * GROUP:(t + 1) * GROUP, :], hl_copied, T_G + t + 1)\
                    .then_inc(psum_free, 1)
                splits(b, LATE)
            product(NG - 1)
            product_lo(NG - 1)
            splits(b, LATE + 1, NEXT)

            def add_turn(half, b, rows, n):
                dve.wait_ge(mm_done, b + BLOCKS)
                dve.tensor_tensor(acc[:, rows, :], acc[:, rows, :], banks(half)[:, :, 0:T], ALU.add)\
                   .then_inc(acc_half, 1)
                dve.wait_ge(acc_half, n + 1)
                dve.tensor_tensor(acc[:, rows, :], acc[:, rows, :], banks(half)[:, :, T:2 * T], ALU.add)\
                   .then_inc(psum_free, 1)

            def last_pair(b, use, n0, free, n, end=False):
                rows = [slice(g * GROUP, (g + 1) * GROUP) for g in range(NG)]
                dve.wait_ge(psum_free, free)
                dve.wait_ge(acc_ready, NG * use + NG)
                dve.tensor_reduce(ln_sum, acc[:, 0:2 * GROUP, :].rearrange("p c t -> p t c"), AX_X, ALU.add)\
                   .then_inc(ln_part, 1)
                splits(b, START, START + 2)
                dve.wait_ge(ln_mm, 3 * n + 1)
                dve.tensor_scalar(ln_shift, ps[:, 4, 0:T], float(NC) / (2 * GROUP), None, ALU.mult)\
                   .then_inc(ln_shifted, 1)
                dve.wait_ge(ln_shifted, n + 1)
                dve.scalar_tensor_tensor(out=ln_sum, in0=ln_shift, scalar=-2.0 * GROUP, in1=ln_sum,
                                         op0=ALU.mult, op1=ALU.add).then_inc(ln_link, 1)
                for g in range(NG):
                    if g == 2:
                        splits(b, START + 2, START + 3)
                    dve.tensor_tensor(acc[:, rows[g], :], acc[:, rows[g], :],
                                      ln_shift.unsqueeze(1).to_broadcast([P, GROUP, T]), ALU.subtract)\
                       .then_inc(ln_centred if g < 2 else ln_late, 1)
                splits(b, START + 3, LATE)
                dve.wait_ge(ln_late, 2 * n + 2)
                add_turn(0, b, rows[2], n0)
                splits(b, LATE, NEXT)
                b += BLOCKS
                dve.wait_ge(psum_free, free + 1)
                dve.tensor_reduce(ln_sum4, acc[:, rows[2], :].rearrange("p c t -> p t c"), AX_X, ALU.add)\
                   .then_inc(ln_link, 1)
                dve.wait_ge(ln_link, 2 * n + 2)
                dve.tensor_tensor(ln_sum, ln_sum, ln_sum4, ALU.add).then_inc(ln_sums, 1)
                splits(b, START, START + 2)
                dve.wait_ge(sq_added, 2 * n + 2)
                dve.tensor_reduce(ln_sumsq, squares[:, rows[0], :].rearrange("p c t -> p t c"),
                                  AX_X, ALU.add).then_inc(ln_sums, 1)
                splits(b, START + 2, BLOCKS if end else BLOCKS + 2)
                for k, (first, last) in enumerate(PIECES):
                    if k < 2:
                        dve.wait_ge(piece_mm, 2 * n + k + 1)
                    else:
                        dve.wait_ge(mm_done, b + BLOCKS)
                    piece = slice(rows[3].start + first, rows[3].start + last)
                    dve.tensor_tensor(acc[:, piece, :], acc[:, piece, :], banks(1)[:, first:last, 0:T], ALU.add)\
                       .then_inc(piece_half, 1)
                    dve.wait_ge(piece_half, 3 * n + k + 1)
                    dve.tensor_tensor(acc[:, piece, :], acc[:, piece, :],
                                      banks(1)[:, first:last, T:2 * T], ALU.add)\
                       .then_inc(piece_added if k < 2 else psum_free, 1)

                dve.wait_ge(psum_free, free + 2)
                dve.wait_ge(ln_sqmean, n + 1)
                dve.wait_ge(ln_mm, 3 * n + 3)
                if end:
                    mean_sq, squared, var, std, rstd = ps[:, 2:4, 0:1], tok[:, 1], tok[:, 2], tok[:, 3], tok[:, 4]
                else:
                    mean_sq, squared, var, std, rstd = ps[:, 1, 0:T], ln_sqm, ln_var_t, ln_std, ln_rstd
                dve.tensor_tensor(var, mean_sq, squared, ALU.subtract).then_inc(ln_var, 1)
                dve.wait_ge(ln_copied, n + 1)
                if not end:
                    dve.tensor_tensor(acc[:, 0:2, :], acc[:, 0:2, :],
                                      ln_mean.unsqueeze(1).to_broadcast([P, 2, T]), ALU.subtract)\
                       .then_inc(ln_zero, 1)
                dve.wait_ge(ln_root, n + 1)
                dve.reciprocal(rstd, std).then_inc(ln_inv, 1)
                dve.wait_ge(ln_inv, n + 1)
                if end:
                    norm_tokens()
                    return

                def scale(k):
                    if k == 0:
                        dve.wait_ge(ln_zero, n + 1)
                    else:
                        dve.wait_ge(ln_zero_p, (STEPS - 1) * n + k)
                    for c in (2 * k, 2 * k + 1):
                        col = C_LNG + n * NC + c
                        dve.scalar_tensor_tensor(out=acc[:, c, :], in0=acc[:, c, :], scalar=prm[:, col:col + 1],
                                                 in1=ln_rstd, op0=ALU.mult, op1=ALU.mult).then_inc(ln_scaled, 1)

                def lo(k):
                    for c in (2 * k, 2 * k + 1):
                        dve.wait_ge(ln_hi, n * NC + c + 1)
                        col = C_LNB + n * NC + c
                        ins = dve.scalar_tensor_tensor(out=xin[:, c, 1, :], in0=acc[:, c, :],
                                                       scalar=prm[:, col:col + 1], in1=xin[:, c, 0, :],
                                                       op0=ALU.add, op1=ALU.subtract)
                    ins.then_inc(pair_ready, 1)

                scale(0)
                lo(0)
                scale(1)
                for k in range(1, STEPS):
                    if k + 1 < STEPS:
                        scale(k + 1)
                    lo(k)
                    if k in (1, 2, 4, 5):
                        off = BLOCKS + 2 + (1, 2, 4, 5).index(k)
                        splits(b, off, off + 1)

            def norm_tokens():
                dve.scalar_tensor_tensor(out=tok[:, 5], in0=tok[:, 0], scalar=-1.0, in1=tok[:, 4],
                                         op0=ALU.mult, op1=ALU.mult).then_inc(tok_bias, 1)
                dve.wait_ge(rows_loaded, 32)
                n = 0
                for k, (g, h, who) in enumerate(UNITS):
                    if who == "dve":
                        cols = slice(g * COLS, (g + 1) * COLS)
                        dve.wait_ge(out_t, k + 1)
                        dve.scalar_tensor_tensor(out=out_tok[:, h, cols], in0=out_bank(g, h),
                                                 scalar=tok[:, 0, h, :], in1=gain_row[:, cols],
                                                 op0=ALU.subtract, op1=ALU.mult).then_inc(out_link, 1)
                        n += 1
                        dve.wait_ge(out_link, n)
                        dve.scalar_tensor_tensor(out=out_tok[:, h, cols], in0=out_tok[:, h, cols],
                                                 scalar=tok[:, 4, h, :], in1=bias_row[:, cols],
                                                 op0=ALU.mult, op1=ALU.add).then_inc(out_dve, 1)
                for k, (g, h, who) in enumerate([unit for unit in UNITS if unit[2] != "dve"]):
                    if who == "both":
                        cols = slice(g * COLS, (g + 1) * COLS)
                        dve.wait_ge(out_link_p, k + 1)
                        dve.tensor_tensor(out_tok[:, h, cols], out_tok[:, h, cols], bias_row[:, cols], ALU.add)\
                           .then_inc(out_dve, 1)

            def out_unit(b0, use, n0, free, n):
                for t in range(2):
                    b = b0 + t * BLOCKS
                    splits(b, START, LATE)
                    dve.wait_ge(acc_ready, NG * use + t + 1)
                    add_turn(t, b, slice(t * GROUP, (t + 1) * GROUP), n0 + t)
                    splits(b, LATE, NEXT)
                last_pair(b0 + 2 * BLOCKS, use, n0 + 2, free + 2, n)

            def mlp(b0, sq, use, n0, free, n, end=False):
                def w1_turns(s, h):
                    for j in range(2):
                        b = b0 + s * SLAB_BLOCKS + h * (2 * BLOCKS) + j * BLOCKS
                        m = sq + s * NG + h * 2 + j
                        rows = bass.ds(h * (2 * GROUP) + j * GROUP, GROUP)
                        splits(b, START, LATE)
                        add_hh(j, e1[:, :, :], sq_hl, m + 1).then_inc(psum_free, 1)
                        dve.wait_ge(psum_free, free + s * (2 * NG) + h * 2 + (j + 1))
                        dve.scalar_tensor_tensor(out=e2[:, :, :], in0=e1[:, :, :], scalar=0.0, in1=e1[:, :, :],
                                                 op0=ALU.max, op1=ALU.mult).then_inc(sq_val, 1)
                        splits(b, LATE, LATE + 1)
                        dve.wait_ge(sq_hi, m + 1)
                        dve.tensor_tensor(hid[:, rows, 1, :], e2[:, :, :], hid[:, rows, 0, :], ALU.subtract)\
                           .then_inc(pair_ready, 2)
                        splits(b, LATE + 1, NEXT)

                def w2_turns(s, h):
                    for j in range(2):
                        b = b0 + NG * BLOCKS + s * SLAB_BLOCKS + h * (2 * BLOCKS) + j * BLOCKS
                        splits(b, START, LATE)
                        dve.wait_ge(acc_ready, NG * use + NG)
                        add_turn(j, b, bass.ds(h * (2 * GROUP) + j * GROUP, GROUP),
                                 n0 + s * NG + h * 2 + j)
                        splits(b, LATE, NEXT)

                with dve.Fori(0, SLABS - 1) as s:
                    with dve.Fori(0, NG // 2) as h:
                        w1_turns(s, h)
                    with dve.Fori(0, NG // 2) as h:
                        w2_turns(s, h)
                s = SLABS - 1
                with dve.Fori(0, NG // 2) as h:
                    w1_turns(s, h)
                w2_turns(s, 0)
                last_pair(b0 + NG * BLOCKS + s * SLAB_BLOCKS + 2 * BLOCKS, use, n0 + s * NG + 2,
                          free + s * 2 * NG + NG + 2, n, end)

            out_unit(B_RO, 0, 0, T_RO, 0)
            mlp(B_MLP0, 0, 1, NG - 1, T_MLP0, 1)

            cos_t = ropet[:, 0:1, :].to_broadcast([32, GROUP, T])
            sin_t = ropet[:, 1:2, :].to_broadcast([32, GROUP, T])
            swap = [k ^ ROPE_HALF for k in range(32)]
            dve.wait_ge(consts, 6)
            with dve.Fori(0, NG // 2) as it:
                for j in range(2):
                    g = it * 2 + j
                    b = B_QKV + it * (6 * BLOCKS) + j * (3 * BLOCKS)
                    for part, dst in enumerate((qg, kg)):
                        splits(b + part * BLOCKS, START, LATE)
                        links = it * 12 + 6 * j + 3 * part
                        n = it * 4 + 2 * j + part
                        add_hh((j, 1 - j)[part], dst, hl_copied, T_RO + n + 1).then_inc(qk_link, 1)
                        dve.wait_ge(qk_link, links + 1)
                        dve.tensor_tensor(cosd[0:32, :, :], dst[0:32, :, :], cos_t, ALU.mult)
                        dve.stream_shuffle(rot[0:32, :, :], dst[0:32, :, :], swap).then_inc(qk_link, 1)
                        dve.wait_ge(qk_link, links + 2)
                        dve.tensor_tensor(rot[0:32, :, :], rot[0:32, :, :], sin_t, ALU.mult)\
                           .then_inc(qk_link, 1)
                        dve.wait_ge(qk_link, links + 3)
                        splits(b + part * BLOCKS, LATE, LATE + 1)
                        dve.tensor_tensor(dst[0:32, :, :], cosd[0:32, :, :], rot[0:32, :, :], ALU.add)\
                           .then_inc(qk_ready, 1)
                        splits(b + part * BLOCKS, LATE + 1, NEXT)
                    bv = b + 2 * BLOCKS
                    al = it * 6 + 3 * j
                    splits(bv, START, AHEAD + 3)
                    dve.wait_ge(scores_done, g + 1)
                    dve.tensor_tensor(prob, banks(1 - j)[:, :, 0:3 * P],
                                      maskt[:, :].unsqueeze(1).to_broadcast([P, GROUP, 3 * P]), ALU.add)\
                       .then_inc(att_link, 1)
                    dve.wait_ge(att_link, al + 1)
                    dve.tensor_reduce(stat[:, :, 0:1], prob[:, :, 0:P], AX_X, ALU.max)
                    dve.tensor_reduce(stat[:, :, 1:2], prob[:, :, P:3 * P], AX_X, ALU.max)\
                       .then_inc(att_link, 1)
                    dve.wait_ge(att_link, al + 2)
                    dve.tensor_scalar(stat[:, :, 2:4], stat[:, :, 0:2], -QK_SCALE, None, ALU.mult)\
                       .then_inc(bias_ready, 1)
                    splits(bv, AHEAD + 3, AHEAD + 4)
                    dve.wait_ge(exp_done, g + 1)
                    dve.reciprocal(stat[:, :, 6:8], stat[:, :, 4:6]).then_inc(att_link, 1)
                    dve.wait_ge(att_link, al + 3)
                    dve.tensor_tensor(prob[:, :, 0:P], prob[:, :, 0:P],
                                      stat[:, :, 6:7].to_broadcast([P, GROUP, P]), ALU.mult)
                    dve.tensor_tensor(prob[:, :, P:3 * P], prob[:, :, P:3 * P],
                                      stat[:, :, 7:8].to_broadcast([P, GROUP, 2 * P]), ALU.mult)\
                       .then_inc(p_ready, 1)
                    splits(bv, AHEAD + 4, LATE)
                    dve.wait_ge(pv_hi, g + 1)
                    rows = bass.ds(g * GROUP, GROUP)
                    dve.tensor_tensor(hid[:, rows, 1, :],
                                      banks(j)[:, 2:4, :].rearrange("p b (c t) -> p (b c) t", t=T),
                                      hid[:, rows, 0, :], ALU.subtract).then_inc(pair_ready, 2)
                    splits(bv, LATE, NEXT)
            out_unit(B_MO, 2, (NG - 1) + (SLABS * NG - 1), T_MO, 2)
            mlp(B_MLP1, SLABS * NG, 3, 2 * (NG - 1) + (SLABS * NG - 1), T_MLP1, 3, end=True)


_INS = ["x", "ln_g", "ln_b", "mlp_w1", "mlp_w2", "rg_w_in", "rg_conv_w", "rg_conv_b", "rg_gate_a_w",
        "rg_gate_a_b", "rg_gate_x_w", "rg_gate_x_b", "rg_lambda", "rg_w_out", "moba_w_qkv", "moba_w_out"]


def rope_table():
    inv = np.float32(500000.0) ** (-np.arange(0, 32, 2, dtype=np.float32) / np.float32(32))
    ang = np.arange(T, dtype=np.float32)[None, :] * inv.astype(np.float32)[:, None]
    cos, sin = np.cos(ang).astype(np.float32), np.sin(ang).astype(np.float32)
    return np.stack([np.concatenate([cos, cos]), np.concatenate([-sin, sin])], axis=1)


def kernel(**inputs):
    import concourse.bacc as _bacc
    from concourse.bass_utils import run_bass_kernel_spmd as _run

    nc = _bacc.Bacc("TRN2", target_bir_lowering=False, num_devices=1)
    arrays, args = {}, []
    given = {n: inputs[n] for n in _INS}
    given["rope"] = rope_table()
    for name, value in given.items():
        a = np.ascontiguousarray(value)
        arrays[f"in_{name}_dram"] = a
        args.append(nc.dram_tensor(f"in_{name}_dram", a.shape, mybir.dt.from_np(a.dtype),
                                   kind="ExternalInput").ap())
    out = nc.dram_tensor("out_dram", (1, T, D), F32, kind="ExternalOutput").ap()
    build_trunk(nc, *args, out)
    r = _run(nc, [arrays], core_ids=[0])
    return r.results[0]["out_dram"]
```
